# Optimizing a Trainium2 kernel written in Bass

```python
import math
import jax, jax.numpy as jnp
from jax import lax
import numpy as np

D_MODEL = 1024
BATCH = 1
SEQ = 128
DEPTH = 2
DEC_BATCH = 1
DEC_SEQ = 1024
PAST_LEN = 128

GRID_W = 64
N_HEADS = 8
N_KV_HEADS = 2
HEAD_DIM = 64
ATTN_WIDTH = N_HEADS * HEAD_DIM
KV_WIDTH = N_KV_HEADS * HEAD_DIM
POOL_WIDTH = D_MODEL - ATTN_WIDTH
POOL_WINDOWS = (2, 4, 8, 16)
N_POOL_GROUPS = len(POOL_WINDOWS)
POOL_GROUP = POOL_WIDTH // N_POOL_GROUPS
FOURIER_WIDTH = D_MODEL // 4
N_FOURIER_GROUPS = 4
FOURIER_GROUP = FOURIER_WIDTH // N_FOURIER_GROUPS
CONV_WIDTH = D_MODEL - FOURIER_WIDTH
CONV_K = 3
D_FF = 2816
FFN_CONV_K = 3
ROPE_THETA = 10000.0
Q_BLOCK = 128
LN_EPS = 1e-6
RMS_EPS = 1e-6
N_EVEN = (DEPTH + 1) // 2
N_ODD = DEPTH // 2
N_ATTN_LAYERS = N_EVEN
IN_EVEN = ATTN_WIDTH + 2 * KV_WIDTH + POOL_WIDTH
IN_ODD = 3 * CONV_WIDTH + FOURIER_WIDTH
DEEPNORM_ALPHA = (2 * DEPTH) ** 0.25
DEEPNORM_BETA = (8 * DEPTH) ** -0.25

kernel_name = 'hybrid_diffusion_prefix_trunk_step'

def layer_norm(x, g=None, b=None):
    xf = x.astype(jnp.float32)
    mu = jnp.mean(xf, -1, keepdims=True)
    var = jnp.mean(jnp.square(xf - mu), -1, keepdims=True)
    y = (xf - mu) * lax.rsqrt(var + LN_EPS)
    if g is not None:
        y = y * g.astype(jnp.float32) + b.astype(jnp.float32)
    return y.astype(x.dtype)

def rms_norm(x, g):
    xf = x.astype(jnp.float32)
    y = xf * lax.rsqrt(jnp.mean(xf * xf, -1, keepdims=True) + RMS_EPS) * g.astype(jnp.float32)
    return y.astype(x.dtype)

def axial_rope_tables(L):
    rows = L // GRID_W
    row = jnp.repeat(jnp.arange(rows, dtype=jnp.float32), GRID_W)
    col = jnp.tile(jnp.arange(GRID_W, dtype=jnp.float32), rows)
    n_freq = HEAD_DIM // 4
    inv = 1.0 / (ROPE_THETA ** (jnp.arange(n_freq, dtype=jnp.float32) / n_freq))
    ang = jnp.concatenate([row[:, None] * inv, col[:, None] * inv], -1)
    return jnp.cos(ang), jnp.sin(ang)

def apply_rope(x, cos, sin):
    xp = x.astype(jnp.float32).reshape(x.shape[:-1] + (HEAD_DIM // 2, 2))
    x0, x1 = xp[..., 0], xp[..., 1]
    c = cos[None, :, None, :]
    s = sin[None, :, None, :]
    out = jnp.stack([x0 * c - x1 * s, x0 * s + x1 * c], -1)
    return out.reshape(x.shape).astype(x.dtype)

def block_attention(q, k, v):
    B, Lq = q.shape[0], q.shape[1]
    nb = Lq // Q_BLOCK
    G = N_HEADS // N_KV_HEADS
    qb = q.reshape(B, nb, Q_BLOCK, N_KV_HEADS, G, HEAD_DIM).transpose(1, 0, 2, 3, 4, 5)
    scale = HEAD_DIM ** -0.5

    def one_block(qblk):
        s = jnp.einsum('bqkgd,bskd->bkgqs', qblk, k).astype(jnp.float32) * scale
        p = jax.nn.softmax(s, axis=-1).astype(v.dtype)
        return jnp.einsum('bkgqs,bskd->bqkgd', p, v)

    o = lax.map(one_block, qb)
    return o.transpose(1, 0, 2, 3, 4, 5).reshape(B, Lq, ATTN_WIDTH)

def centred_mean_pool(u, w):
    B, L, C = u.shape
    cs = jnp.concatenate([jnp.zeros((B, 1, C), jnp.float32), jnp.cumsum(u.astype(jnp.float32), axis=1)], 1)
    t = jnp.arange(L)
    lo = jnp.clip(t - w // 2, 0, L)
    hi = jnp.clip(t + w // 2, 0, L)
    s = cs[:, hi] - cs[:, lo]
    cnt = (hi - lo).astype(jnp.float32)
    return (s / cnt[None, :, None]).astype(u.dtype)

def pool_mixer(p, w_pool, pool_scale):
    B, L, _ = p.shape
    grp = p.reshape(B, L, N_POOL_GROUPS, POOL_GROUP)
    pooled = jnp.stack([centred_mean_pool(grp[:, :, i], w) for i, w in enumerate(POOL_WINDOWS)], 2) - grp
    mixed = jnp.einsum('blgc,gcd->blgd', pooled, w_pool)
    return mixed.reshape(B, L, POOL_WIDTH) * pool_scale

def depthwise_conv(x, w, b):
    K = w.shape[0]
    pad = K // 2
    L = x.shape[1]
    xp = jnp.pad(x, ((0, 0), (pad, K - 1 - pad), (0, 0)))
    y = b
    for j in range(K):
        y = y + xp[:, j:j + L] * w[j]
    return y

def fourier_mix(f):
    B, L, _ = f.shape
    fg = f.reshape(B, L, N_FOURIER_GROUPS, FOURIER_GROUP).astype(jnp.float32)
    out = jnp.fft.fft2(fg, axes=(1, 3), norm='ortho').real
    return out.reshape(B, L, FOURIER_WIDTH).astype(f.dtype)

def even_mixer(u, w_in, q_g, k_g, w_pool, pool_scale, rope, ctx_k, ctx_v):
    B, L, _ = u.shape
    proj = u @ w_in
    o1 = ATTN_WIDTH
    o2 = o1 + KV_WIDTH
    o3 = o2 + KV_WIDTH
    q = rms_norm(proj[..., :o1].reshape(B, L, N_HEADS, HEAD_DIM), q_g)
    k = rms_norm(proj[..., o1:o2].reshape(B, L, N_KV_HEADS, HEAD_DIM), k_g)
    v = proj[..., o2:o3].reshape(B, L, N_KV_HEADS, HEAD_DIM)
    p = proj[..., o3:]
    if rope is None:
        attn = block_attention(q, k, v)
    else:
        cos, sin = rope
        qr = apply_rope(q, cos, sin)
        kr = apply_rope(k, cos, sin)
        attn = block_attention(qr, jnp.concatenate([kr, ctx_k], 1), jnp.concatenate([v, ctx_v], 1))
    pool = pool_mixer(p, w_pool, pool_scale)
    return jnp.concatenate([attn, pool], -1), k, v

def odd_mixer(u, w_in, conv_w, conv_b):
    proj = u @ w_in
    h = proj[..., :CONV_WIDTH]
    bg = proj[..., CONV_WIDTH:2 * CONV_WIDTH]
    cg = proj[..., 2 * CONV_WIDTH:3 * CONV_WIDTH]
    f = proj[..., 3 * CONV_WIDTH:]
    conv_out = bg * depthwise_conv(cg * h, conv_w, conv_b)
    return jnp.concatenate([conv_out, fourier_mix(f)], -1)

def conv_ffn(u, w_up, cw, cb, w_down):
    a, g = jnp.split(u @ w_up, 2, axis=-1)
    return (jax.nn.silu(depthwise_conv(a, cw, cb)) * g) @ w_down

def run_trunk(x, cond, ctx_k, ctx_v, w_ada, b_ada, w_in_even, q_norm_g, k_norm_g, w_pool, pool_scale,
              w_in_odd, conv_w, conv_b, w_out, w_up, ffn_conv_w, ffn_conv_b, w_down, ln_g, ln_b):
    is_latent = ctx_k is not None
    rope = axial_rope_tables(x.shape[1]) if is_latent else None
    new_k, new_v = [], []
    for l in range(DEPTH):
        ada = jax.nn.silu(cond) @ w_ada[l] + b_ada[l]
        sh1, sc1, g1, sh2, sc2, g2 = jnp.split(ada[:, None, :], 6, axis=-1)
        u = layer_norm(x) * (1 + sc1) + sh1
        if l % 2 == 0:
            e = l // 2
            m, k, v = even_mixer(u, w_in_even[e], q_norm_g[e], k_norm_g[e], w_pool[e], pool_scale[e], rope,
                                 ctx_k[:, e] if is_latent else None, ctx_v[:, e] if is_latent else None)
            if not is_latent:
                new_k.append(k)
                new_v.append(v)
        else:
            o = l // 2
            m = odd_mixer(u, w_in_odd[o], conv_w[o], conv_b[o])
        x = layer_norm(DEEPNORM_ALPHA * x + g1 * (m @ w_out[l]), ln_g[l, 0], ln_b[l, 0])
        u = layer_norm(x) * (1 + sc2) + sh2
        f = conv_ffn(u, w_up[l], ffn_conv_w[l], ffn_conv_b[l], w_down[l])
        x = layer_norm(DEEPNORM_ALPHA * x + g2 * f, ln_g[l, 1], ln_b[l, 1])
    return x, new_k, new_v

def setup_inputs(seed: int = 0) -> dict:
    key = jax.random.key(seed)
    ks = iter(jax.random.split(key, 32))

    def nrm(shape, scale):
        return jax.random.normal(next(ks), shape, jnp.float32) * scale

    D = D_MODEL
    return {
        'x_prompt': nrm((BATCH, SEQ, D), 1.0),
        'x_sample': nrm((DEC_BATCH, DEC_SEQ, D), 1.0),
        'cache_k': nrm((DEC_BATCH, N_ATTN_LAYERS, PAST_LEN, N_KV_HEADS, HEAD_DIM), 1.0),
        'cache_v': nrm((DEC_BATCH, N_ATTN_LAYERS, PAST_LEN, N_KV_HEADS, HEAD_DIM), 1.0),
        'c': nrm((DEC_BATCH, D), 1.0),
        'c_ctx': nrm((D,), 1.0),
        'w_ada': nrm((DEPTH, D, 6 * D), D ** -0.5),
        'b_ada': nrm((DEPTH, 6 * D), 0.02),
        'w_in_even': nrm((N_EVEN, D, IN_EVEN), D ** -0.5),
        'q_norm_g': 1.0 + nrm((N_EVEN, HEAD_DIM), 0.02),
        'k_norm_g': 1.0 + nrm((N_EVEN, HEAD_DIM), 0.02),
        'w_pool': nrm((N_EVEN, N_POOL_GROUPS, POOL_GROUP, POOL_GROUP), POOL_GROUP ** -0.5),
        'pool_scale': 1.0 + nrm((N_EVEN, POOL_WIDTH), 0.02),
        'w_in_odd': nrm((N_ODD, D, IN_ODD), D ** -0.5),
        'conv_w': nrm((N_ODD, CONV_K, CONV_WIDTH), CONV_K ** -0.5),
        'conv_b': nrm((N_ODD, CONV_WIDTH), 0.02),
        'w_out': nrm((DEPTH, D, D), D ** -0.5 * DEEPNORM_BETA),
        'w_up': nrm((DEPTH, D, 2 * D_FF), D ** -0.5),
        'ffn_conv_w': nrm((DEPTH, FFN_CONV_K, D_FF), FFN_CONV_K ** -0.5),
        'ffn_conv_b': nrm((DEPTH, D_FF), 0.02),
        'w_down': nrm((DEPTH, D_FF, D), D_FF ** -0.5 * DEEPNORM_BETA),
        'ln_g': 1.0 + nrm((DEPTH, 2, D), 0.02),
        'ln_b': nrm((DEPTH, 2, D), 0.02),
    }

def reference(x_prompt, x_sample, cache_k, cache_v, c, c_ctx, w_ada, b_ada, w_in_even, q_norm_g, k_norm_g,
              w_pool, pool_scale, w_in_odd, conv_w, conv_b, w_out, w_up, ffn_conv_w, ffn_conv_b, w_down,
              ln_g, ln_b):
    y_prompt, ks, vs = run_trunk(x_prompt, c_ctx[None, :], None, None, w_ada, b_ada, w_in_even, q_norm_g,
                                 k_norm_g, w_pool, pool_scale, w_in_odd, conv_w, conv_b, w_out, w_up,
                                 ffn_conv_w, ffn_conv_b, w_down, ln_g, ln_b)
    new_cache_k = jnp.stack(ks, 1)
    new_cache_v = jnp.stack(vs, 1)
    y_sample, _, _ = run_trunk(x_sample, c, cache_k, cache_v, w_ada, b_ada, w_in_even, q_norm_g, k_norm_g,
                               w_pool, pool_scale, w_in_odd, conv_w, conv_b, w_out, w_up, ffn_conv_w,
                               ffn_conv_b, w_down, ln_g, ln_b)
    return (y_prompt, y_sample, new_cache_k, new_cache_v)


_drawn_inputs = setup_inputs


def setup_inputs(seed=0):
    import zlib

    import numpy as np

    out = dict(_drawn_inputs(seed))
    spreads = {}
    factors = {'cache_k': 8.0,
     'cache_v': 8.0,
     'q_norm_g': 8.0,
     'pool_scale': 25.532,
     'conv_b': 8.0,
     'ffn_conv_b': 8.0}
    for name, (base, spread) in spreads.items():
        noise = np.random.default_rng([zlib.crc32(name.encode()), seed]).standard_normal(out[name].shape)
        drawn = base * np.exp(spread * noise) if base else spread * noise
        out[name] = __import__('jax').numpy.asarray(drawn.astype(out[name].dtype))
    for name, factor in factors.items():
        out[name] = (out[name] * factor).astype(out[name].dtype)
    return out
```

```python
from contextlib import ExitStack

import numpy as np

import concourse.bass as bass
from concourse import mybir

F32 = mybir.dt.float32
F32R = mybir.dt.float32r
ALU = mybir.AluOpType
ACT = mybir.ActivationFunctionType
AX_X = mybir.AxisListType.X

P = 128
D = 1024
KD = D // P
CTX, LAT, PAST = 128, 1024, 128
TOK = CTX + LAT
NT = TOK // P
NQ = LAT // P
CH = 384
NCH = TOK // CH
HD, NH, NKV = 64, 8, 2
G = NH // NKV
AW = NH * HD
QK = AW + NKV * HD
IN_E = AW + 2 * NKV * HD + (D - AW)
NPG = 4
WINDOWS = (2, 4, 8, 16)
CW = 768
CB = CW // P
FW = D - CW
FB = FW // P
DFF = 2816
NF = DFF // P
NG = NF // 2
ALPHA = 4.0 ** 0.25
EPS = 1e-6
PADW = TOK + 4
PIECES = [[(0, CTX, 1), (CTX, CH - CTX, CTX + 2)]] + [[(c * CH, CH, c * CH + 2)] for c in range(1, NCH)]
PPW = TOK + 24
PPIECES = [[(0, CTX, 8), (CTX, CH - CTX, CTX + 16)]] + [[(c * CH, CH, c * CH + 16)] for c in range(1, NCH)]
NKEY = LAT + PAST + CTX
LKB = (LAT + PAST) // P

U_POOL, U_FFN0, U_FOUR, U_CONV, U_FFN1 = 0, 4, 4 + 4 * NG, 6 + 4 * NG, 24 + 4 * NG
D_ADA0 = 0
D_QKV = D_ADA0 + 4 * 16
D_WPOOL = D_QKV + 8
D_OUT0 = D_WPOOL + 1
D_DOWN0 = D_OUT0 + 8
D_ADA1 = D_DOWN0 + NF
D_CHAN = D_ADA1 + 4 * 8
D_CTAB = D_CHAN + 1
D_TAB = D_CTAB + 1
D_OUT1 = D_TAB + 16
D_DOWN1 = D_OUT1 + 8
CHUNKS = (0, 1, 3, 4)


def ada_half(m):
    if m < 6:
        return 0, m
    if m < 10:
        return 1, m - 6
    return (0, m - 4) if m < 16 else (1, m - 12)


def ada_steps(kind):
    if kind == "in":
        return {s: [4 + 2 * s, 5 + 2 * s] if s < 3 else [7 + s] for s in range(9)}
    return {s: [15 + s] for s in range(1, 9)} if kind == "end0" else {}



C_ID, C_EDGE, C_SELC, C_SELB, C_EPS, NCON = 0, 128, 192, 194, 450, 452


def constants():
    con = np.zeros((P, NCON), np.float32)
    con[:, C_ID:C_ID + P] = np.eye(P)
    for g, w in enumerate(WINDOWS):
        for j in range(8):
            con[:, C_EDGE + 16 * g + j] = w / (min(j + w // 2, CTX) - max(j - w // 2, 0))
            t = CTX - 8 + j
            con[:, C_EDGE + 16 * g + 8 + j] = w / (min(t + w // 2, CTX) - max(t - w // 2, 0))
    for cond in range(2):
        for r in (cond, 2):
            con[r, C_SELC + cond] = 1
            con[r, C_SELB + P * cond:C_SELB + P * (cond + 1)] = 1
    con[:, C_EPS] = EPS
    n_freq = HD // 4
    inv = 1.0 / (10000.0 ** (np.arange(n_freq) / n_freq))
    t = np.arange(LAT)
    ang = np.concatenate([(t // 64)[:, None] * inv, (t % 64)[:, None] * inv], -1)
    rope = np.zeros((LAT, 2, HD // 2, 2))
    rope[:, 0] = np.cos(ang)[:, :, None]
    rope[:, 1, :, 0], rope[:, 1, :, 1] = -np.sin(ang), np.sin(ang)
    a = 2 * np.pi * np.outer(np.arange(64), np.arange(64)) / 64
    chan = np.zeros((P, 2, P))
    for b in range(2):
        s = slice(64 * b, 64 * b + 64)
        chan[s, 0, s], chan[s, 1, s] = np.cos(a) / 8, np.sin(a) / 8

    def table(n):
        a = 2 * np.pi * (np.outer(np.arange(n), np.arange(n)) % n) / n
        return np.cos(a) / np.sqrt(n), -np.sin(a) / np.sqrt(n)

    cc, cs = table(CTX)
    lc, ls = table(LAT)
    pos = np.stack([lc.reshape(8, P, LAT), ls.reshape(8, P, LAT)], 1)
    f = np.float32
    return {"k_con": con, "k_rope": rope.reshape(LAT, 2 * HD).astype(f), "k_chan": chan.reshape(P, 2 * P).astype(f),
            "k_ctab": np.concatenate([cc, cs], 1).astype(f), "k_pos": pos.reshape(16, P, LAT).astype(f)}


def build(nc, t):
    ctx = ExitStack()
    with ctx:
        base = (nc.sbuf_base + 31) // 32 * 32
        REG = 8 * 2 * TOK * 4
        off_a, off_b = base, base + REG
        off_c = base + 2 * REG

        def at(name, shape, dt, off):
            return nc.alloc_sbuf_tensor_at(name, shape, dt, offset=off)

        def size(shape):
            n = 4
            for x in shape[1:]:
                n *= x
            return (n + 31) // 32 * 32

        end = [off_c]

        def fixed(name, shape, dt=F32):
            r = at(name, shape, dt, end[0])
            end[0] += size(shape)
            return r

        act_a = at("act_a", [P, KD, 2, TOK], F32R, off_a)
        act_b = at("act_b", [P, KD, 2, TOK], F32R, off_b)
        con = fixed("con", [P, NCON])
        cols = fixed("cols", [P, 2, 4, KD, 2])
        par = fixed("par", [P, 220])
        conds = fixed("conds", [P, KD, 2])
        fgrp = fixed("fgrp", [P, 4, 2])
        stats = fixed("stats", [P, 3, 48])
        small = fixed("small", [P, 64])
        off_raw_u = end[0]
        raw_u = fixed("raw_u", [P, 2, KD, P])
        raw_d = fixed("raw_d", [P, 2, D])
        off_uw = end[0]
        uw = fixed("uw", [P, 2, 2, KD, P], F32R)
        off_s = end[0]
        dw = at("dw", [P, 2, 2, D], F32R, off_s)
        ident = con[:, C_ID:C_ID + P]
        eps = con[:, C_EPS:C_EPS + 1]
        ln_y = at("ln_y", [P, 3, D], F32, off_s)
        ln_t = at("ln_t", [P, D], F32, off_s + 12288)
        ln_z = at("ln_z", [P, D], F32, off_s + 16384)
        ln_u = at("ln_u", [P, D], F32, off_s + 20480)
        ln_g = at("ln_g", [P, D], F32, off_s + 24576)
        ada_row = at("ada_row", [P, 3, 512], F32, off_s + 28672)
        bias_row = [at(f"bias_row{i}", [P, D], F32, off_s + 20480 + 4096 * i) for i in range(2)]
        prow = at("prow", [P, 4, P], F32, off_b + 16384)
        kt = at("kt", [P, NKV, NKEY], F32R, off_s)
        vhl = at("vhl", [P, NKEY // P, NKV, 2, HD], F32R, off_s + 10240)
        q_ctx = at("q_ctx", [P, NH, HD], F32, off_s + 20480)
        k4 = at("k4", [P, NKV, 2, HD], F32, off_s + 22528)
        xn = at("xn", [P, NH + NKV, HD], F32, off_s + 23552)
        rope_a = at("rope_a", [P, NH + NKV, HD], F32, off_s + 26112)
        rope_b = at("rope_b", [P, NH + NKV, HD], F32, off_s + 28672)
        sq = at("sq", [P, NH + NKV, HD], F32, off_s + 31232)
        rope_t = at("rope_t", [P, 2, 2, HD], F32, off_s + 33792)
        kv_out = at("kv_out", [P, 2, P], F32, off_s + 34816)
        kv_past = at("kv_past", [P, 2, P], F32, off_s + 35840)
        g_row = at("g_row", [P, 2, HD], F32, off_s + 36864)
        pool_t2 = at("pool_t2", [P, PPW], F32, off_s + 37376)
        pool_t1 = at("pool_t1", [P, PPW], F32, off_raw_u)
        xk = at("xk", [P, NKV, HD], F32, off_s + 42112)
        wp = at("wp", [P, 2, NPG, P], F32R, off_s + 24576)
        mf = at("mf", [P, TOK], F32, off_s + 28672)
        wq = at("wq", [P, KD, 2, AW], F32R, off_b)
        wkv = at("wkv", [P, KD, 2, 2 * NKV * HD], F32R, off_uw)
        pp = at("pp", [P, NPG, PPW], F32, off_b + 36864)
        q_lat = at("q_lat", [P, NQ, AW], F32, off_b + 36864 + 18816)
        pt = at("pt", [P, 2, LKB, G, P], F32R, off_a)
        prob = at("prob", [P, 4, LAT + PAST], F32, off_a + 36864)
        qs = at("qs", [P, G, 2, 2, HD], F32, off_a + 55296)
        qt = at("qt", [P, 2, G, 2, P], F32R, off_a + 59392)
        o_t = at("o_t", [P, G, P], F32, off_a + 67584)
        o_f = at("o_f", [P, 2, P], F32, off_a + 69632)
        ph = at("ph", [P, NPG, 2, TOK], F32R, off_a + 36864)
        wo = [at(f"wo{l}", [P, KD, 2, D], F32R, o) for l, o in enumerate((off_a, off_b))]
        gb_mid = [at(f"gbm{l}", [P, 2, D], F32, o + 65536) for l, o in enumerate((off_a, off_b))]
        gb_end = [at(f"gbe{l}", [P, 2, D], F32, o + 36864) for l, o in enumerate((off_a, off_b))]
        acc = [at(f"acc{l}", [P, NT, D], F32, o) for l, o in enumerate((off_a, off_b))]
        hh = [at(f"hh{l}", [P, 2, 2, TOK], F32R, o + 36864) for l, o in enumerate((off_a, off_b))]
        f_t = [at(f"ft{l}", [P, PADW], F32, o + 55296) for l, o in enumerate((off_a, off_b))]
        f_s = [at(f"fs{l}", [P, PADW], F32, o + 55296 + 4640) for l, o in enumerate((off_a, off_b))]
        f_h = [at(f"fh{l}", [P, PADW], F32, o + 55296 + 9280) for l, o in enumerate((off_a, off_b))]
        f_a = at("fa", [P, PADW], F32, off_s + 16384)
        f_in = at("f_in", [P, FB, 2, TOK], F32R, off_a)
        f_ch = at("f_ch", [P, NT, 2, 2 * FW], F32R, off_a + 18432)
        chan = at("chan", [P, 2, 2 * P], F32R, off_s + 16384)
        c_h = at("c_h", [P, TOK], F32, off_s + 16384 + 2048)
        c_p = at("c_p", [P, PADW], F32, off_s + 16384 + 2048 + 4608)
        c_t = at("c_t", [P, PADW], F32, off_s + 16384 + 2048 + 9248)
        c_m = at("c_m", [P, TOK], F32, off_s + 16384 + 2048 + 13888)

        ps = ctx.enter_context(nc.psum_tensor("ps", [P, 8, 512], F32))

        sems = {}

        def sem(name):
            sems[name] = ctx.enter_context(nc.semaphore(name))
            return sems[name]

        s_con = sem("s_con")
        setup_t, setup_c = sem("setup_t"), sem("setup_c")
        u_loaded = [sem(f"u_loaded{i}") for i in range(2)]
        u_hi, u_split, up_done = sem("u_hi"), sem("u_split"), sem("up_done")
        bank_free = [sem(f"bank_free{i}") for i in range(2)]
        d_loaded = [sem(f"d_loaded{i}") for i in range(2)]
        d_hi, d_split, d_used = sem("d_hi"), sem("d_split"), sem("d_used")
        ada_bank = sem("ada_bank")
        ada_st = [sem(f"ada_st{i}") for i in range(3)]
        brow = [sem(f"brow{i}") for i in range(2)]
        brow_mm, cols_done = sem("brow_mm"), sem("cols_done")
        x_ld = [sem(f"x_ld{i}") for i in range(3)]
        x_st = [sem(f"x_st{i}") for i in range(3)]
        gb_ld, gate_ld, gate_mm, gate_rdy = sem("gb_ld"), sem("gate_ld"), sem("gate_mm"), sem("gate_rdy")
        out_done, out_evac = sem("out_done"), sem("out_evac")
        stat1, sd1, rs1, norm1, x1_rdy = (sem(x) for x in ("stat1", "sd1", "rs1", "norm1", "x1_rdy"))
        stat2, sd2, rs2, z_rdy = (sem(x) for x in ("stat2", "sd2", "rs2", "z_rdy"))
        zt_done, mod_done, act_hi, act_rdy = (sem(x) for x in ("zt_done", "mod_done", "act_hi", "act_rdy"))
        v_step, g_step = sem("v_step"), sem("g_step")
        pp_zero, pool_done = sem("pp_zero"), sem("pool_done")
        g_ld, past_ld = sem("g_ld"), sem("past_ld")
        rope_ld = [sem(f"rope_ld{i}") for i in range(2)]
        qkv_done, qkv_free = sem("qkv_done"), sem("qkv_free")
        sq_done, ss_done, qsd, k_rdy, k_hi, k_lo = (sem(x) for x in ("sq_done", "ss_done", "qsd", "k_rdy", "k_hi", "k_lo"))
        kt_tr, kt_ev, v_hi, v_out, kv_st = (sem(x) for x in ("kt_tr", "kt_ev", "v_hi", "v_out", "kv_st"))
        qs_hi, qs_lo, qt_tr = (sem(x) for x in ("qs_hi", "qs_lo", "qt_tr"))
        s_done, mx_done, exp_done, rinv_done, p_rdy = (sem(x) for x in ("s_done", "mx_done", "exp_done", "rinv_done", "p_rdy"))
        tr_done, th_hi = sem("tr_done"), sem("th_hi")
        t_free = [sem(f"t_free{i}") for i in range(2)]
        pv_done, o_cp, o_sum, m_hi, m_att = (sem(x) for x in ("pv_done", "o_cp", "o_sum", "m_hi", "m_att"))
        ph_hi, ph_lo, mix_done, mix_ev, mix_hi, mix_lo = (sem(x) for x in ("ph_hi", "ph_lo", "mix_done", "mix_ev", "mix_hi", "mix_lo"))
        pads, acc_zero = sem("pads"), sem("acc_zero")
        conv_done, silu_done, h_mul, h_hi, h_rdy = (sem(x) for x in ("conv_done", "silu_done", "h_mul", "h_hi", "h_rdy"))
        down_done, down_added = sem("down_done"), sem("down_added")
        fi_hi, fc_done, fc_hi, fc_lo, pos_hi, pos_lo = (sem(x) for x in (
            "fi_hi", "fc_done", "fc_hi", "fc_lo", "pos_hi", "pos_lo"))
        ch_rdy, cp_rdy, cm_rdy, cm_hi, cm_lo = (sem(x) for x in ("ch_rdy", "cp_rdy", "cm_rdy", "cm_hi", "cm_lo"))
        g_mul = sem("g_mul")

        CREDITS = [(u_split, 2), (up_done, 6), (bank_free[0], 3), (bank_free[1], 3), (d_split, 2), (d_used, 2),
                   (ada_bank, 3), (ada_st[0], 16), (ada_st[1], 16), (ada_st[2], 16), (conv_done, 1), (silu_done, 1), (h_mul, 3),
                   (down_added, 2), (cp_rdy, 3), (cm_rdy, 3), (t_free[0], 1), (t_free[1], 1)]

        xs = t["xs"]
        ada = t["ada"]

        w_conv = t["w_in_odd"][0].rearrange("(k p) n -> p k n", p=P)

        def dram_rows(ap, tile):
            return ap[bass.ds(tile * P, P), :]

        def u_source(n, f=None):
            if f is not None:
                l, gate = n
                w, col = t["w_up"][l], gate * DFF + f * P
            elif n < U_FFN0:
                w, col = t["w_in_even"][0], QK + NKV * HD + n * P
            elif n < U_CONV:
                w, col = t["w_in_odd"][0], 3 * CW + (n - U_FOUR) * P
            return w.rearrange("(k p) n -> p k n", p=P)[:, :, bass.ds(col, P)]

        LN = {"in": dict(ph=0, i1=None, i4=0, im=None), "mid0": dict(ph=1, i1=0, i4=1, im=0),
              "end0": dict(ph=2, i1=1, i4=2, im=None), "mid1": dict(ph=3, i1=2, i4=3, im=1),
              "end1": dict(ph=4, i1=3, i4=None, im=None)}

        def ada_stored(eng, n):
            for s in range(3):
                eng.wait_ge(ada_st[s], 16 + 16 * len(range(s, n, 3)))

        class Step:
            def __init__(self, base, i=None):
                self.base, self.i = base, i

            def tile(self, lag):
                return self.base - lag if self.i is None else self.i * 3 + (self.base - lag)

            def third(self, lag):
                return (self.base - lag) // 3 if self.i is None else self.i + (self.base - lag) // 3

            def slot(self, lag):
                return (self.base - lag) % 3

            def live(self, lag):
                return self.i is not None or 0 <= self.base - lag < NT

            def first(self, lag):
                return self.i is None and self.base == lag

        def ln_steps(eng, step, loop=lambda i: None):
            for s in range(3):
                step(Step(s))
            with eng.Fori(0, 2) as i:
                loop(i)
                for s in range(3, 6):
                    step(Step(s, i))
            loop(None)
            for s in range(9, 11):
                step(Step(s))

        def t_uses(ctx_tile, last):
            order = [("q", 0, 0), ("q", 0, 1)] if ctx_tile else []
            for s in range(1, 9):
                nxt = (s - 1) // 4 + 1
                if s % 4 == 1 and not (nxt > 1 and (ctx_tile or last)):
                    order += [("q", nxt, 0), ("q", nxt, 1)]
                order += [("t", s - 1, r) for r in range(1 if ctx_tile else 3)]
                if (s - 1) % 4 == 3:
                    order += [("o", (s - 1) // 4, 0)]
            return {u: n for n, u in enumerate(order)}

        class QTile:
            def __init__(self, q, last=False):
                self.q, self.last, self.ctx = q, last, q is None
                self.uses = t_uses(self.ctx, last)
                first_latent = len(t_uses(True, False)) + 2
                self.half = 0 if self.ctx else q * (len(t_uses(False, False)) // 2) + first_latent // 2
                self.rounds = 1 if self.ctx else 3
                self.nk = 1 if self.ctx else LKB
                self.head0 = 0 if self.ctx else q * NH + NH
                self.unit0 = 0 if self.ctx else q * 2 + 2
                self.round0 = 0 if self.ctx else q * (3 * NH) + NH
                self.key0 = LAT + PAST if self.ctx else 0

            def loc(self, use):
                if use[0] == "q" and use[1] == 0 and not self.ctx:
                    return use[2] - 2
                return self.uses[use]

            def wait_bank(self, eng, loc):
                eng.wait_ge(t_free[loc % 2], self.half + (loc // 2 + 1))

            def wait_evac(self, eng, loc):
                eng.wait_ge(t_free[loc % 2], self.half + (loc // 2 + 2))

        assert len(t_uses(True, False)) % 2 == 0 and len(t_uses(False, False)) % 2 == 0

        def att_steps(eng, step, first, loop=lambda i: None):
            c = QTile(None)
            first(c)
            for s in range(-1, 9):
                step(c, s)
            q0 = QTile(0)
            first(q0)
            for s in (-1, 0):
                step(q0, s)
            with eng.Fori(0, NQ - 1) as q:
                loop(q)
                tile = QTile(q)
                for s in range(1, 9):
                    step(tile, s)
            loop(None)
            tile = QTile(NQ - 1, last=True)
            for s in range(1, 9):
                step(tile, s)

        def has_score(tile, s):
            return s + 1 < NH or not (tile.ctx or tile.last)

        def has_trans(s):
            return 0 <= s - 1 < NH

        def turns_queries(tile, s):
            return s in (1, 5) and not (s == 5 and (tile.ctx or tile.last))

        def rounds_queries(tile, s):
            return s in (0, 4, 8) and not (s > 0 and (tile.ctx or tile.last))

        def conv_unit(i, e):
            return i * 6 + (U_CONV + e), i * 3 + (U_CONV // 2 + e // 2), e % 2

        block = ctx.enter_context(nc.Block())

        @block.sync
        def _(sp):
            sp.dma_start(con[:], t["k_con"]).then_inc(s_con, 16)
            sp.dma_start(prow[0:8, 3, :], t["c"].rearrange("a (k p) -> (a k) p", p=P)).then_inc(s_con, 16)
            sp.dma_start(prow[8:16, 3, :], t["c_ctx"].rearrange("(k p) -> k p", p=P)).then_inc(s_con, 16)
            for l in range(2):
                sp.dma_start(prow[0:66, l, :], t["ffn_conv_w"][l].rearrange("j (k p) -> (j k) p", p=P)).then_inc(s_con, 16)
                sp.dma_start(prow[66:88, l, :], t["ffn_conv_b"][l:l + 1].rearrange("a (k p) -> (a k) p", p=P)).then_inc(s_con, 16)
            sp.dma_start(prow[0:18, 2, :], t["conv_w"][0].rearrange("j (k p) -> (j k) p", p=P)).then_inc(s_con, 16)
            sp.dma_start(prow[18:24, 2, :], t["conv_b"].rearrange("a (k p) -> (a k) p", p=P)).then_inc(s_con, 16)
            sp.dma_start(prow[24:28, 2, :], t["pool_scale"].rearrange("a (k p) -> (a k) p", p=P)).then_inc(s_con, 16)

            def d_unit(n, src, width=D):
                sp.wait_ge(d_split, n + 1)
                sp.dma_start(raw_d[:, n % 2, 0:width], src).then_inc(d_loaded[n % 2], 16)

            def ada_units(m, i=None):
                l, half = ada_half(m)
                col = half * 512 if i is None else i * 1536 + half * 512
                n = 4 * m if m < 16 else D_ADA1 + 4 * (m - 16)
                w = t["w_ada"][l].rearrange("(u kk p) n -> u p kk n", kk=2, p=P)
                for u in range(4):
                    sp.wait_ge(d_split, n + u + 1 if i is None else i * 12 + (n + u + 1))
                    sp.dma_start(raw_d[:, (n + u) % 2, :].rearrange("p (kk n) -> p kk n", kk=2), w[u][:, :, bass.ds(col, 512)]).then_inc(d_loaded[(n + u) % 2], 16)

            def bias_rows(ns, stored):
                ada_stored(sp, stored)
                if stored > 4:
                    sp.wait_ge(act_rdy, NT if stored == 16 else 3 * NT)
                for n in ns:
                    l, j = n // 4, CHUNKS[n % 4]
                    if n >= 2:
                        sp.wait_ge(brow_mm, n - 1)
                    sp.dma_start(bias_row[n % 2][0:2, :], ada[l, :, j * D:(j + 1) * D]).then_inc(brow[n % 2], 16)
                    sp.dma_start(bias_row[n % 2][2:3, :], t["b_ada"][l:l + 1, j * D:(j + 1) * D]).then_inc(brow[n % 2], 16)

            for m in range(4):
                ada_units(m)
            bias_rows(range(2), 4)

            def ln_loads(kind, src, dst=None):
                i1, i4 = LN[kind]["i1"], LN[kind]["i4"]

                def load(tile, slot):
                    sp.dma_start(ln_y[:, slot, :], dram_rows(src, tile)).then_inc(x_ld[slot], 16)

                if i1 is not None:
                    l, m = (0 if kind.endswith("0") else 1), (0 if kind.startswith("mid") else 1)
                    j = (2, 5)[m]
                    sp.dma_start(ln_u[0:2, :], ada[l, :, j * D:(j + 1) * D]).then_inc(gate_ld, 16)
                    sp.dma_start(ln_u[2:3, :], t["b_ada"][l:l + 1, j * D:(j + 1) * D]).then_inc(gate_ld, 16)
                for s in range(3):
                    load(s, s)
                if i1 is not None:
                    gb = (gb_mid, gb_end)[m][l]
                    sp.dma_start(gb[:, 0, :], t["ln_g"][l, m, :].partition_broadcast(P)).then_inc(gb_ld, 16)
                    sp.dma_start(gb[:, 1, :], t["ln_b"][l, m, :].partition_broadcast(P)).then_inc(gb_ld, 16)

                for s in range(3):
                    for m in ada_steps(kind).get(s, []):
                        ada_units(m)

                def step(tile, slot, used):
                    if i1 is not None:
                        sp.wait_ge(x1_rdy, tile + (NT * i1 + 1))
                        sp.dma_start(dram_rows(dst, tile), ln_y[:, slot, :]).then_inc(x_st[slot], 16)
                    if used is not None:
                        if i4 is not None:
                            sp.wait_ge(z_rdy, tile + (NT * i4 + 1))
                        if i1 is not None:
                            sp.wait_ge(x_st[slot], used * 16 + 48 * i1)
                        load(tile + 3, slot)

                with sp.Fori(0, 2) as i:
                    for j in range(3):
                        step(i * 3 + j, j, i + 1)
                        for m in ada_steps(kind).get(3 + j, []):
                            ada_units(m, i)
                for j in range(3):
                    step(6 + j, j, None)
                if i1 is not None:
                    for j in range(3):
                        sp.wait_ge(x_st[j], 48 * (i1 + 1))

            ln_loads("in", t["x_all"])

            def u_unit(n, src):
                sp.wait_ge(u_split, n + 1)
                sp.dma_start(raw_u[:, n % 2, :, :], src).then_inc(u_loaded[n % 2], 16)

            for n in range(U_POOL, U_FFN0):
                u_unit(n, u_source(n))
            bias_rows(range(2, 6), 16)
            sp.dma_start(g_row[:, 0, :], t["q_norm_g"][0].partition_broadcast(P)).then_inc(g_ld, 16)
            sp.dma_start(g_row[:, 1, :], t["k_norm_g"][0].partition_broadcast(P)).then_inc(g_ld, 16)
            sp.dma_start(kv_past[:, 0, :], t["cache_k"][0, 0].rearrange("s h d -> s (h d)")).then_inc(past_ld, 16)
            sp.dma_start(kv_past[:, 1, :], t["cache_v"][0, 0].rearrange("s h d -> s (h d)")).then_inc(past_ld, 16)
            for i in range(2):
                sp.dma_start(rope_t[:, i, :, :], t["k_rope"][i * P:(i + 1) * P].rearrange("t (a d) -> t a d", a=2)).then_inc(rope_ld[i], 16)
            for k in range(KD):
                d_unit(D_QKV + k, t["w_in_even"][0][k * P:(k + 1) * P, 0:QK + NKV * HD], QK + NKV * HD)
            sp.wait_ge(d_split, D_WPOOL + 1)
            sp.dma_start(raw_d[:, D_WPOOL % 2, 0:NPG * P].rearrange("p (g d) -> p g d", g=NPG),
                         t["w_pool"][0].rearrange("g c d -> c g d")).then_inc(d_loaded[D_WPOOL % 2], 16)
            sp.wait_ge(k_rdy, 1)
            sp.dma_start(t["new_k"][0, 0].rearrange("s h d -> s (h d)"), kv_out[:, 0, :]).then_inc(kv_st, 16)
            sp.wait_ge(v_out, 1)
            sp.dma_start(t["new_v"][0, 0].rearrange("s h d -> s (h d)"), kv_out[:, 1, :]).then_inc(kv_st, 16)
            with sp.Fori(0, NQ // 2 - 1) as i:
                for j in range(2):
                    sp.wait_ge(k_rdy, i * 2 + (j + 2))
                    sp.dma_start(rope_t[:, j, :, :], dram_rows(t["k_rope"], i * 2 + (j + 2))
                                 .rearrange("t (a d) -> t a d", a=2)).then_inc(rope_ld[j], 16)

            def out_units(l, d0):
                for k in range(KD):
                    d_unit(d0 + k, t["w_out"][l][k * P:(k + 1) * P, :])

            class FfnLoads:
                def __init__(self, l, u0, d0):
                    self.l, self.u0, self.d0 = l, u0, d0

                def u(self, g, j):
                    sp.wait_ge(u_split, g * 4 + (self.u0 + j + 1))
                    sp.dma_start(raw_u[:, j % 2, :, :], u_source((self.l, j % 2), g * 2 + j // 2)).then_inc(u_loaded[j % 2], 16)

                def dn(self, g, j):
                    sp.wait_ge(d_split, g * 2 + (self.d0 + j + 1))
                    sp.dma_start(raw_d[:, (self.d0 + j) % 2, :], dram_rows(t["w_down"][self.l], g * 2 + j)).then_inc(
                        d_loaded[(self.d0 + j) % 2], 16)

                def rest(self):
                    with sp.Fori(0, NG - 1) as g:
                        self.u(g, 2)
                        self.u(g, 3)
                        self.u(g + 1, 0)
                        self.dn(g + 1, 0)
                        self.dn(g + 1, 1)
                        self.u(g + 1, 1)
                    self.u(NG - 1, 2)
                    self.u(NG - 1, 3)

            out_units(0, D_OUT0)
            sp.wait_ge(pool_done, 1)
            f = FfnLoads(0, U_FFN0, D_DOWN0)
            f.u(0, 0)
            f.u(0, 1)
            sp.wait_ge(mix_lo, NPG)
            ln_loads("mid0", t["x_all"], xs[0])
            f.dn(0, 0)
            f.dn(0, 1)
            f.rest()
            for n in (U_FOUR, U_FOUR + 1):
                u_unit(n, u_source(n))
            sp.wait_ge(down_done, 18 * NG)
            ln_loads("end0", xs[0], xs[1])
            d_unit(D_CHAN, t["k_chan"], 2 * P)
            d_unit(D_CTAB, t["k_ctab"], 2 * P)
            bias_rows(range(6, 8), 24)
            u_unit(U_CONV, w_conv[:, :, 0:P])
            for k in range(16):
                d_unit(D_TAB + k, t["k_pos"][k])
            with sp.Fori(0, CB // 2 - 1) as i:
                for e in range(1, 7):
                    n, _h, slot = conv_unit(i, e)
                    sp.wait_ge(u_split, n + 1)
                    sp.dma_start(raw_u[:, slot, :, :], w_conv[:, :, bass.ds(i * (2 * P) + ((0, 2 * CW, CW)[e % 3] + e // 3 * P), P)]).then_inc(u_loaded[slot], 16)
            for e in range(1, 6):
                n = U_CONV + 6 * (CB // 2 - 1) + e
                col = (0, 2 * CW, CW)[e % 3] + (CB - 2 + e // 3) * P
                u_unit(n, w_conv[:, :, col:col + P])
            f = FfnLoads(1, U_FFN1, D_DOWN1)
            f.u(0, 0)
            f.u(0, 1)
            out_units(1, D_OUT1)
            ln_loads("mid1", xs[1], xs[2])
            f.dn(0, 0)
            f.dn(0, 1)
            f.rest()
            sp.wait_ge(down_done, 36 * NG)
            ln_loads("end1", xs[2], t["y_all"])
            sp.wait_ge(kv_st, 32)

        @block.gpsimd
        def _(gp):
            for s, v in CREDITS:
                gp.sem_inc(s, v)
            gp.memset(pp[:], 0.0).then_inc(pp_zero, 1)
            chained = [0]

            def chain(ins):
                chained[0] += 1
                ins.then_inc(g_step, 1)
                gp.wait_ge(g_step, chained[0])

            gp.wait_ge(bank_free[0], 3 + 6)
            gp.wait_ge(bank_free[1], 3 + 6)
            for g, w in enumerate(WINDOWS):
                bufs, i, width, first, last = (pool_t1, pool_t2), 0, 2, 1, PPW
                chain(gp.tensor_tensor(bufs[0][:, 1:PPW], pp[:, g, 0:PPW - 1], pp[:, g, 1:PPW], ALU.add))
                while width < w:
                    h = width // 2
                    cur, nxt = bufs[i % 2], bufs[(i + 1) % 2]
                    first, last = first + h, last - h
                    chain(gp.tensor_tensor(nxt[:, first:last], cur[:, first - h:last - h], cur[:, first + h:last + h], ALU.add))
                    width, i = width * 2, i + 1
                cur, nxt = bufs[i % 2], bufs[(i + 1) % 2]
                for start, n in ((8, CTX), (CTX + 16, LAT)):
                    for j, e in ((0, 0), (n - 8, 8)):
                        c = cur[:, start + j:start + j + 8]
                        chain(gp.tensor_tensor(c, c, con[:, C_EDGE + 16 * g + e:C_EDGE + 16 * g + e + 8], ALU.mult))
                for j, (start, n) in enumerate(((8, CTX), (CTX + 16, LAT))):
                    chain(gp.tensor_scalar(nxt[:, start:start + n], cur[:, start:start + n], 1.0 / w, 0.0, ALU.mult, ALU.add))
                    o = gp.tensor_tensor(pp[:, g, start:start + n], nxt[:, start:start + n], pp[:, g, start:start + n], ALU.subtract)
                    if g == NPG - 1 and j == 1:
                        o.then_inc(pool_done, 1)
                    else:
                        chain(o)

            def step(tile, s):
                if has_score(tile, s):
                    h = s + 1
                    i = tile.head0 + h
                    gp.wait_ge(rinv_done, i + 1)
                    sl = prob[:, h % 4, 0:tile.nk * P]
                    gp.tensor_tensor(sl, sl, small[:, 16 + h % 4:17 + h % 4].broadcast_to([P, tile.nk * P]), ALU.mult).then_inc(p_rdy, 1)

            att_steps(gp, step, lambda tile: None)

            def ln_affine(kind):
                i1 = LN[kind]["i1"]
                gb = (gb_mid if kind.startswith("mid") else gb_end)[0 if kind.endswith("0") else 1]
                gp.wait_ge(gb_ld, 32 * (i1 + 1))

                def step(s):
                    if s.live(0):
                        gp.wait_ge(norm1, s.tile(0) + (NT * i1 + 1))
                        y = ln_y[:, s.slot(0), :]
                        gp.tensor_tensor(y, y, gb[:, 0, :], ALU.mult).then_inc(g_mul, 1)
                        gp.wait_ge(g_mul, s.tile(0) + (NT * i1 + 1))
                        gp.tensor_tensor(y, y, gb[:, 1, :], ALU.add).then_inc(x1_rdy, 1)
                ln_steps(gp, step)

            def clear_acc(l):
                gp.wait_ge(out_done, NT * (l + 1))
                gp.memset(acc[l][:], 0.0).then_inc(acc_zero, 1)

            def clear_pads(line, after):
                gp.wait_ge(act_rdy, after)
                gp.memset(line[:, 0:1], 0.0)
                gp.memset(line[:, CTX + 1:CTX + 2], 0.0)
                gp.memset(line[:, PADW - 2:PADW], 0.0).then_inc(pads, 1)

            ln_affine("mid0")
            clear_acc(0)
            clear_pads(f_a, 2 * NT)
            ln_affine("end0")
            gp.wait_ge(brow_mm, 8)
            clear_pads(c_p, 3 * NT)
            ln_affine("mid1")
            clear_acc(1)
            clear_pads(f_a, 4 * NT)
            ln_affine("end1")

        @block.scalar
        def _(act):
            def copy(o, i):
                return act.activation(o, i, ACT.Copy)

            act.wait_ge(setup_t, 4)
            copy(par[:], ps[:, 0, 0:220]).then_inc(setup_c, 1)
            act.activation(conds[:].rearrange("p k c -> p c k"), ps[:, 0, 204:220].rearrange("p (c k) -> p c k", c=2), ACT.Silu).then_inc(setup_c, 1)

            def d_hi_at(slot, count, dst, width=D):
                act.wait_ge(d_loaded[slot], count * 16)
                copy(dst, raw_d[:, slot, 0:width]).then_inc(d_hi, 1)

            def ada_evac(m, i=None):
                l, half = ada_half(m)
                used = (4 * m if m < 16 else D_ADA1 + 4 * (m - 16)) + 6
                col = half * 512 if i is None else i * 1536 + half * 512
                act.wait_ge(d_split, used if i is None else i * 12 + used)
                act.wait_ge(ada_st[m % 3], 16 * (m // 3 + 1) if i is None else i * 16 + 16 * (m // 3 + 1))
                copy(ada_row[0:2, m % 3, :], ps[0:2, m % 3, :]).then_inc(ada_bank, 1)
                act.wait_ge(ada_bank, m + 4 if i is None else i * 3 + (m + 4))
                act.dma_start(ada[l, :, bass.ds(col, 512)], ada_row[0:2, m % 3, :]).then_inc(ada_st[m % 3], 16)

            for m in range(4):
                ada_evac(m)

            def ln_act(kind, dest):
                i1, i4 = LN[kind]["i1"], LN[kind]["i4"]
                l = 0 if kind in ("in", "mid0") else 1
                c0 = 0 if kind in ("in", "end0") else 2

                def gate(k):
                    act.wait_ge(gate_mm, 2 * i1 + k)
                    if k == 2:
                        act.wait_ge(out_evac, NT * i1 + 1)
                    copy(ln_g[:].rearrange("p (a n) -> p a n", a=2), ps[:, 6:8, :]).then_inc(gate_rdy, 1)

                def step(s):
                    if i4 is not None and s.live(2):
                        tile = s.tile(2)
                        cc = 1 if s.first(2) else 0
                        act.wait_ge(zt_done, tile + (NT * i4 + 1))
                        if not s.first(2):
                            act.wait_ge(act_rdy, tile + NT * i4)
                        for k in range(KD):
                            o = act.activation(ln_u[:, k * P:(k + 1) * P], ps[:, 6 + k // 4, (k % 4) * P:(k % 4 + 1) * P],
                                               ACT.Identity, bias=cols[:, l, c0, k, cc:cc + 1], scale=cols[:, l, c0 + 1, k, cc:cc + 1])
                        o.then_inc(mod_done, 1)
                        act.wait_ge(mod_done, tile + (NT * i4 + 1))
                        copy(dest[:, :, 0, bass.ds(tile * P, P)], ln_u[:].rearrange("p (k t) -> p k t", k=KD)).then_inc(act_hi, 1)
                    if i1 is not None and s.live(0):
                        if s.first(0):
                            gate(2)
                        st = stats[:, s.slot(0), :]
                        act.wait_ge(stat1, s.tile(0) + (NT * i1 + 1))
                        act.activation(st[:, 14:15], st[:, 13:14], ACT.Sqrt, bias=eps, scale=1.0).then_inc(sd1, 1)
                        act.wait_ge(rs1, s.tile(0) + (NT * i1 + 1))
                        y = ln_y[:, s.slot(0), :]
                        act.activation(y, y, ACT.Identity, bias=st[:, 16:17], scale=st[:, 15:16]).then_inc(norm1, 1)
                    if i4 is not None and s.live(1):
                        tile = s.tile(1)
                        st = stats[:, s.slot(1), :]
                        act.wait_ge(stat2, tile + (NT * i4 + 1))
                        act.activation(st[:, 34:35], st[:, 33:34], ACT.Sqrt, bias=eps, scale=1.0).then_inc(sd2, 1)
                        act.wait_ge(rs2, tile + (NT * i4 + 1))
                        if not s.first(1):
                            act.wait_ge(zt_done, tile + NT * i4)
                        act.activation(ln_z[:], ln_y[:, s.slot(1), :], ACT.Identity, bias=st[:, 36:37], scale=st[:, 35:36]).then_inc(z_rdy, 1)
                    for m in ada_steps(kind).get(s.base, []):
                        ada_evac(m, s.i)

                if i1 is not None:
                    gate(1)
                ln_steps(act, step)

            act.wait_ge(cols_done, 2)
            ln_act("in", act_a)

            def u_hi_at(n, half, slot):
                act.wait_ge(u_loaded[slot], half * 16 + 16)
                act.wait_ge(up_done, n * 3 + 3)
                copy(uw[:, slot, 0, :, :], raw_u[:, slot, :, :]).then_inc(u_hi, 1)

            act.wait_ge(pp_zero, 1)
            u_hi_at(0, 0, 0)
            for n in range(NPG):
                if n + 1 < NPG:
                    u_hi_at(n + 1, (n + 1) // 2, (n + 1) % 2)
                for c in range(NCH):
                    act.wait_ge(up_done, 6 + 3 * n + c + 1)
                    for u0, ln, p0 in PPIECES[c]:
                        o = copy(pp[:, n, p0:p0 + ln], ps[:, 3 * (n % 2) + c, u0 - c * CH:u0 - c * CH + ln])
                    o.then_inc(bank_free[n % 2], 1)

            act.wait_ge(up_done, 6 + 12)
            for k in range(KD):
                n = D_QKV + k
                act.wait_ge(d_loaded[n % 2], 16 * (n // 2 + 1))
                copy(wq[:, k, 0, :], raw_d[:, n % 2, 0:AW])
                copy(wkv[:, k, 0, :], raw_d[:, n % 2, AW:AW + 256]).then_inc(d_hi, 1)

            def heads(ap):
                return ap.rearrange("p (h d) -> p h d", d=HD)

            def k_round(src):
                copy(k4[:, :, 0, :].bitcast(F32R), src).then_inc(k_hi, 1)

            def kt_evac(idx, kb, bank):
                act.wait_ge(kt_tr, idx + 1)
                copy(kt[:, :, bass.ds(kb * P, P)], ps[:, 4 + bank, 0:256].rearrange("p (v t) -> p v t", v=2)).then_inc(kt_ev, 1)

            def qkv_tile(tile, par2, ctx_tile):
                qb, vb = 2 * par2, 2 * par2 + 1
                act.wait_ge(qkv_done, tile + 1)
                if not ctx_tile:
                    act.wait_ge(k_rdy, tile)
                act.activation(sq[:, 0:NH, :], heads(ps[:, qb, :]), ACT.Square)
                act.activation(sq[:, NH:, :], heads(ps[:, vb, 0:P]), ACT.Square).then_inc(sq_done, 1)
                if ctx_tile:
                    copy(kv_out[:, 1, :], ps[:, vb, P:2 * P]).then_inc(v_out, 1)
                kb = LKB if ctx_tile else tile - 1
                copy(vhl[:, bass.ds(kb, 1), :, 0, :].rearrange("p a v d -> p (a v) d"), heads(ps[:, vb, P:2 * P])).then_inc(v_hi, 1)
                act.wait_ge(ss_done, tile + 1)
                act.activation(small[:, 32:42], small[:, 20:30], ACT.Sqrt, bias=eps, scale=1.0 / HD).then_inc(qsd, 1)
                act.wait_ge(k_rdy, tile + 1)
                if ctx_tile:
                    k_round(heads(kv_out[:, 0, :]))
                    kt_evac(0, LKB, 0)
                    act.wait_ge(past_ld, 32)
                    k_round(heads(kv_past[:, 0, :]))
                    copy(vhl[:, LKB - 1, :, 0, :], heads(kv_past[:, 1, :])).then_inc(v_hi, 1)
                    kt_evac(1, LKB - 1, 1)
                else:
                    k_round(xk[:])
                    kt_evac(tile + 1, tile - 1, 1 - par2)

            qkv_tile(0, 0, True)
            with act.Fori(0, NQ // 2) as i:
                for j in range(2):
                    qkv_tile(i * 2 + (j + 1), 1 - j, False)

            def qs_round(tile, j):
                if not (tile.ctx and j == 0):
                    act.wait_ge(qt_tr, tile.unit0 + j)
                kv = j % 2
                if tile.ctx:
                    src = q_ctx[:, kv * G:(kv + 1) * G, :]
                else:
                    src = q_lat[:, bass.ds(tile.q + j // 2, 1), kv * 256:(kv + 1) * 256].rearrange("p a (h d) -> p (a h) d", h=G)
                copy(qs[:, :, 0, 0, :].bitcast(F32R), src)
                copy(qs[:, :, 0, 1, :].bitcast(F32R), src).then_inc(qs_hi, 1)

            def qt_evac(tile, j):
                act.wait_ge(qt_tr, tile.unit0 + (j + 1))
                for r in range(2):
                    bank = tile.loc(("q", j, r)) % 2
                    copy(qt[:, j % 2, 2 * r:2 * r + 2, :, :].rearrange("p h a t -> p (h a t)"), ps[:, 6 + bank, :]).then_inc(t_free[bank], 1)

            def first(tile):
                if tile.ctx:
                    act.wait_ge(qkv_free, NT)
                qs_round(tile, 0)
                qt_evac(tile, 0)

            def step(tile, s):
                if turns_queries(tile, s):
                    qt_evac(tile, (s - 1) // 4 + 1)
                if has_trans(s):
                    h = s - 1
                    nb = min(3, tile.nk)
                    for r in range(tile.rounds):
                        bank = tile.loc(("t", h, r)) % 2
                        act.wait_ge(tr_done, tile.round0 + (tile.rounds * h + r + 1))
                        copy(pt[:, 0, 3 * r:3 * r + nb, h % 4, :], ps[:, 6 + bank, 0:nb * P].rearrange("p (b t) -> p b t", b=nb)).then_inc(th_hi, 1)
                if has_score(tile, s):
                    h = s + 1
                    act.wait_ge(mx_done, tile.head0 + (h + 1))
                    if tile.ctx:
                        if h >= 4:
                            act.wait_ge(tr_done, h - 3)
                    elif isinstance(tile.q, int) and h < 4:
                        act.wait_ge(tr_done, NH + h - 3)
                    else:
                        act.wait_ge(tr_done, tile.round0 + 3 * (h - 3))
                    nb, nw = (3, CH) if tile.nk > 1 else (1, P)
                    b0 = 3 * (h % 2)
                    act.activation(prob[:, h % 4, 0:nb * nw].rearrange("p (b n) -> p b n", b=nb), ps[:, b0:b0 + nb, 0:nw],
                                   ACT.Exp, bias=small[:, h % 4:h % 4 + 1], scale=1.0, accum_out=small[:, 8 + h % 4:9 + h % 4]).then_inc(exp_done, 1)
                if rounds_queries(tile, s):
                    qs_round(tile, s // 4 + 1)
                if has_trans(s) and (s - 1) % 4 == 3:
                    j = (s - 1) // 4
                    loc = tile.loc(("o", j, 0))
                    act.wait_ge(pv_done, tile.unit0 + (j + 1))
                    copy(o_t[0:HD, :, :], ps[HD:P, 6 + loc % 2, :].rearrange("p (h t) -> p h t", h=G)).then_inc(o_cp, 1)
                    act.wait_ge(o_sum, tile.unit0 + (j + 1))
                    tile.wait_evac(act, loc)
                    tk = 0 if tile.ctx else tile.q + 1
                    copy(act_b[:, 2 * j:2 * j + 2, 0, bass.ds(tk * P, P)], o_f[:]).then_inc(m_hi, 1)

            att_steps(act, step, first)

            act.wait_ge(pool_done, 1)
            act.wait_ge(m_att, 2 + 2 * NQ)
            for g in range(NPG):
                for start, u0, n in ((8, 0, CTX), (CTX + 16, CTX, LAT)):
                    o = copy(ph[:, g, 0, u0:u0 + n], pp[:, g, start:start + n])
                o.then_inc(ph_hi, 1)
            d_hi_at(D_WPOOL % 2, D_WPOOL // 2 + 1, wp[:, 0, :, :].rearrange("p g d -> p (g d)"), NPG * P)

            def wo_hi(l, k, d0):
                d_hi_at((d0 + k) % 2, (d0 + k) // 2 + 1, wo[l][:, k, 0, :])

            for g in range(NPG):
                wo_hi(0, g, D_OUT0)
                act.wait_ge(mix_done, g + 1)
                if g == 0:
                    act.wait_ge(ph_lo, NPG)
                else:
                    act.wait_ge(mix_lo, g)
                act.activation(mf[:].rearrange("p (c n) -> p c n", c=NCH), ps[:, 3 * (g % 2):3 * (g % 2) + 3, 0:CH],
                               ACT.Identity, bias=0.0, scale=par[:, 200 + g:201 + g]).then_inc(mix_ev, 1)
                act.wait_ge(mix_ev, g + 1)
                copy(act_b[:, 4 + g, 0, :], mf[:]).then_inc(mix_hi, 1)
            for k in range(4, KD):
                wo_hi(0, k, D_OUT0)

            class Ffn:
                def __init__(self, l, u0, d0):
                    self.l, self.u0, self.d0 = l, u0, d0

                def hi_u(self, g, j):
                    u_hi_at(g * 4 + (self.u0 + j), g * 2 + (self.u0 // 2 + j // 2), j % 2)

                def body(self, g, last):
                    l, u0, d0 = self.l, self.u0, self.d0
                    hh_, ft, fs, fh = hh[l], f_t[l], f_s[l], f_h[l]
                    for b in range(2):
                        self.hi_u(g, 2 * b + 1)
                        q = g * 2 + (NF * l + b)
                        act.wait_ge(conv_done, q + 1)
                        for c in range(NCH):
                            act.wait_ge(up_done, g * 12 + (6 + 3 * (u0 + 2 * b) + c + 1))
                            for s0, ln, p0 in PIECES[c]:
                                o = copy(f_a[:, p0:p0 + ln], ps[:, c, s0 - c * CH:s0 - c * CH + ln])
                            o.then_inc(bank_free[0], 1)
                        if b == 0:
                            self.hi_u(g, 2)
                            if l or not isinstance(g, int) or g:
                                act.wait_ge(down_done, g * 18 + 18 * NG * l)
                            for j in range(2):
                                d_hi_at((d0 + j) % 2, g + ((d0 + j) // 2 + 1), dw[:, j, 0, :])
                        elif not last:
                            self.hi_u(g + 1, 0)
                        act.wait_ge(conv_done, q + 2)
                        act.wait_ge(h_mul, q * 3 + 3)
                        act.activation(fs[:, 1:PADW - 2], ft[:, 1:PADW - 2], ACT.Silu).then_inc(silu_done, 1)
                        for c in range(NCH):
                            act.wait_ge(h_mul, q * 3 + (c + 4))
                            copy(hh_[:, b, 0, c * CH:(c + 1) * CH], fh[:, c * CH:(c + 1) * CH]).then_inc(h_hi, 1)

                def run(self):
                    for j in range(3):
                        act.wait_ge(x_st[j], 48 * (2 * self.l + 1))
                    act.wait_ge(pads, 1 + 2 * self.l)
                    self.body(0, False)
                    with act.Fori(1, NG - 1) as g:
                        self.body(g, False)
                    self.body(NG - 1, True)

            f = Ffn(0, U_FFN0, D_DOWN0)
            f.hi_u(0, 0)
            act.wait_ge(cols_done, 4)
            ln_act("mid0", act_b)
            f.run()
            u_hi_at(U_FOUR, U_FOUR // 2, 0)
            act.wait_ge(cols_done, 6)
            ln_act("end0", act_b)

            for j in range(3):
                act.wait_ge(x_st[j], 48 * 2)
            act.wait_ge(act_rdy, 3 * NT)
            d_hi_at(D_CHAN % 2, D_CHAN // 2 + 1, chan[:, 0, :], 2 * P)
            u_hi_at(U_FOUR + 1, U_FOUR // 2, 1)
            for b in range(FB):
                if b:
                    u_hi_at(U_CONV, U_CONV // 2, 0)
                for c in range(NCH):
                    act.wait_ge(up_done, 6 + 3 * (U_FOUR + b) + c + 1)
                    copy(f_in[:, b, 0, c * CH:(c + 1) * CH], ps[:, 3 * b + c, 0:CH]).then_inc(fi_hi, 1)
            d_hi_at(D_CTAB % 2, D_CTAB // 2 + 1, dw[:, 0, 0, 0:2 * P], 2 * P)
            for tile in range(NT):
                act.wait_ge(fc_done, tile + 1)
                copy(f_ch[:, tile, 0, :], ps[:, 6 + tile % 2, :]).then_inc(fc_hi, 1)
            for k in range(16):
                act.wait_ge(d_used, 2 + k)
                d_hi_at((D_TAB + k) % 2, (D_TAB + k) // 2 + 1, dw[:, (k + 1) % 2, 0, :])
            for b in range(FB):
                for h in range(3):
                    if b == 0:
                        act.wait_ge(d_used, 3 if h == 0 else 3 + 16)
                    if h == 0:
                        o, i = act_a[:, CB + b, 0, 0:CTX], ps[:, 4 + b, 0:P]
                    else:
                        o, i = act_a[:, CB + b, 0, CTX + 512 * (h - 1):CTX + 512 * h], ps[:, 2 * b + h - 1, :]
                    copy(o, i).then_inc(pos_hi, 1)

            with act.Fori(0, CB // 2) as i:
                for j in range(2):
                    b = i * 2 + j
                    u_hi_at(*conv_unit(i, 3 * j + 1))
                    act.wait_ge(cp_rdy, b * 3 + 3)
                    n = conv_unit(i, 3 * j)[0]
                    for c in range(NCH):
                        act.wait_ge(up_done, n * 3 + (6 + c + 1))
                        copy(c_h[:, c * CH:(c + 1) * CH], ps[:, 3 * j + c, 0:CH]).then_inc(ch_rdy, 1)
                    u_hi_at(*conv_unit(i, 3 * j + 2))
                    u_hi_at(*conv_unit(i, 3 * j + 3))
                    for c in range(NCH):
                        act.wait_ge(cm_rdy, b * 3 + (c + 4))
                        copy(act_a[:, bass.ds(b, 1), 0, c * CH:(c + 1) * CH].rearrange("p a n -> p (a n)"), c_m[:, c * CH:(c + 1) * CH]).then_inc(cm_hi, 1)
            for k in range(KD):
                wo_hi(1, k, D_OUT1)
            act.wait_ge(cols_done, 8)
            ln_act("mid1", act_a)
            Ffn(1, U_FFN1, D_DOWN1).run()
            ln_act("end1", None)

        @block.vector
        def _(v):
            class Chain:
                def __init__(self):
                    self.n, self.i, self.per, self.start = 0, None, 0, 0

                def __call__(self, ins):
                    self.n += 1
                    ins.then_inc(v_step, 1)
                    v.wait_ge(v_step, self.n if self.i is None else self.i * self.per + self.n)

                def enter(self, i, per):
                    self.i, self.per, self.start = i, per, self.n

                def leave(self, passes):
                    assert self.n - self.start == self.per, (self.n - self.start, self.per)
                    self.n, self.i = self.start + passes * self.per, None

            chain = Chain()

            def lo(dst, src, hi):
                return v.tensor_tensor(dst, src, hi.bitcast(F32), ALU.subtract)

            def heads(ap):
                return ap.rearrange("p (h d) -> p h d", d=HD)

            def unsplit(n):
                return 4 * 16 if n < D_ADA1 else 4 * 24

            def d_lo_at(n, slot, dst, hi, width=D, g=None):
                v.wait_ge(d_hi, n + 1 - unsplit(n) if g is None else g * 2 + (n + 1 - unsplit(n)))
                lo(dst, raw_d[:, slot, 0:width], hi).then_inc(d_split, 1)

            def u_lo_at(n, half, slot):
                v.wait_ge(u_hi, n + 1)
                lo(uw[:, slot, 1, :, :], raw_u[:, slot, :, :], uw[:, slot, 0, :, :]).then_inc(u_split, 1)

            def cols_of(ns):
                for n in ns:
                    l, j = n // 4, n % 4
                    v.wait_ge(brow_mm, n + 1)
                    v.tensor_scalar(cols[:, l, j, :, :].rearrange("p k c -> p (k c)"), ps[:, 6 + n % 2, 0:16],
                                    1.0 if j % 2 else 0.0, None, ALU.add).then_inc(cols_done, 1)

            cols_of(range(2))

            def norm_stats(x, st, o):
                for h in range(2):
                    r = v.bn_stats(st[:, o + 6 * h:o + 6 * h + 6], x[:, 512 * h:512 * (h + 1)])
                chain(r)
                v.tensor_copy(st[:, o + 17:o + 19], st[:, o:o + 2])
                return v.bn_aggr(st[:, o + 12:o + 14], st[:, o:o + 12])

            def norm_scale(st, o):
                chain(v.reciprocal(st[:, o + 15:o + 16], st[:, o + 14:o + 15]))
                return v.tensor_scalar(st[:, o + 16:o + 17], st[:, o + 12:o + 13], st[:, o + 15:o + 16], -1.0, ALU.mult, ALU.mult)

            def ln_vec(kind, dest, src):
                ph_, i1, i4, im = (LN[kind][x] for x in ("ph", "i1", "i4", "im"))

                def step(s):
                    if i1 is not None and s.live(0):
                        tile, slot = s.tile(0), s.slot(0)
                        y, st = ln_y[:, slot, :], stats[:, slot, :]
                        if im is not None:
                            v.wait_ge(out_done, tile + (NT * im + 1))
                        if s.first(0):
                            v.wait_ge(gate_rdy, 2 * i1 + 1)
                        if s.i is None and s.base == 1:
                            v.wait_ge(gate_rdy, 2 * i1 + 2)
                        o, x = src(tile, slot)
                        v.tensor_tensor(ln_t[:].rearrange("p (a n) -> p a n", a=o), x, ln_g[:].rearrange("p (a n) -> p a n", a=o), ALU.mult).then_inc(out_evac, 1)
                        v.wait_ge(out_evac, tile + (NT * i1 + 1))
                        v.wait_ge(x_ld[slot], s.third(0) * 16 + (48 * ph_ + 16))
                        chain(v.scalar_tensor_tensor(y, y, ALPHA, ln_t[:], ALU.mult, ALU.add))
                        norm_stats(y, st, 0).then_inc(stat1, 1)
                    if i4 is not None and s.live(2):
                        tile = s.tile(2)
                        v.wait_ge(act_hi, tile + (NT * i4 + 1))
                        lo(dest[:, :, 1, bass.ds(tile * P, P)], ln_u[:].rearrange("p (k t) -> p k t", k=KD), dest[:, :, 0, bass.ds(tile * P, P)]).then_inc(act_rdy, 1)
                    if i1 is not None and s.live(0):
                        v.wait_ge(sd1, s.tile(0) + (NT * i1 + 1))
                        norm_scale(stats[:, s.slot(0), :], 0).then_inc(rs1, 1)
                    if i4 is not None and s.live(1):
                        tile, slot = s.tile(1), s.slot(1)
                        if i1 is not None:
                            v.wait_ge(x1_rdy, tile + (NT * i1 + 1))
                        else:
                            v.wait_ge(x_ld[slot], s.third(1) * 16 + (48 * ph_ + 16))
                        norm_stats(ln_y[:, slot, :], stats[:, slot, :], 20).then_inc(stat2, 1)
                        v.wait_ge(sd2, tile + (NT * i4 + 1))
                        norm_scale(stats[:, slot, :], 20).then_inc(rs2, 1)

                def loop(i):
                    if i is None:
                        chain.leave(2)
                    else:
                        chain.enter(i, 3 * ((3 if i1 is not None else 0) + (2 if i4 is not None else 0)))
                ln_steps(v, step, loop)

            def from_psum(tile, slot):
                return 2, ps[:, 2 * slot:2 * slot + 2, :]

            def from_acc(l):
                return lambda tile, slot: (1, acc[l][:, bass.ds(tile, 1), :])

            ln_vec("in", act_a, None)

            u_lo_at(0, 0, 0)
            for n in range(1, NPG):
                u_lo_at(n, n // 2, n % 2)
            cols_of(range(2, 6))

            for k in range(KD):
                n = D_QKV + k
                v.wait_ge(d_hi, k + 1)
                lo(wq[:, k, 1, :], raw_d[:, n % 2, 0:AW], wq[:, k, 0, :])
                lo(wkv[:, k, 1, :], raw_d[:, n % 2, AW:AW + 256], wkv[:, k, 0, :]).then_inc(d_split, 1)
            v.wait_ge(g_ld, 32)
            chain(v.tensor_scalar(g_row[:, 0, :], g_row[:, 0, :], HD ** -0.5, None, ALU.mult))

            def k_lo_of(idx, src):
                v.wait_ge(k_hi, idx + 1)
                lo(k4[:, :, 1, :].bitcast(F32R), src, k4[:, :, 0, :]).then_inc(k_lo, 1)

            def gains(kind, n):
                return g_row[:, kind, :].unsqueeze(1).broadcast_to([P, n, HD])

            def qkv_tile(tile, par2, ctx_tile, half=None):
                qb, vb = 2 * par2, 2 * par2 + 1
                v.wait_ge(sq_done, tile + 1)
                v.tensor_reduce(small[:, 20:30], sq[:], AX_X, ALU.add).then_inc(ss_done, 1)
                v.wait_ge(qsd, tile + 1)
                chain(v.reciprocal(small[:, 44:54], small[:, 32:42]))
                v.tensor_tensor(xn[:, 0:NH, :], heads(ps[:, qb, :]), small[:, 44:52].unsqueeze(2).broadcast_to([P, NH, HD]), ALU.mult)
                chain(v.tensor_tensor(xn[:, NH:, :], heads(ps[:, vb, 0:P]), small[:, 52:54].unsqueeze(2).broadcast_to([P, NKV, HD]), ALU.mult))
                kb = LKB if ctx_tile else tile - 1
                v.wait_ge(v_hi, 1 if ctx_tile else tile + 2)
                vd = vhl[:, bass.ds(kb, 1), :, :, :]
                lo(vhl[:, bass.ds(kb, 1), :, 1, :].rearrange("p a v d -> p (a v) d"), heads(ps[:, vb, P:2 * P]),
                   vhl[:, bass.ds(kb, 1), :, 0, :].rearrange("p a v d -> p (a v) d")).then_inc(qkv_free, 1)
                if ctx_tile:
                    v.tensor_tensor(q_ctx[:], xn[:, 0:NH, :], gains(0, NH), ALU.mult)
                    v.tensor_tensor(heads(kv_out[:, 0, :]), xn[:, NH:, :], gains(1, NKV), ALU.mult).then_inc(k_rdy, 1)
                    k_lo_of(0, heads(kv_out[:, 0, :]))
                    k_lo_of(1, heads(kv_past[:, 0, :]))
                    v.wait_ge(v_hi, 2)
                    chain(lo(vhl[:, LKB - 1, :, 1, :], heads(kv_past[:, 1, :]), vhl[:, LKB - 1, :, 0, :]))
                    return
                v.tensor_tensor(xn[:, 0:NH, :], xn[:, 0:NH, :], gains(0, NH), ALU.mult)
                chain(v.tensor_tensor(xn[:, NH:, :], xn[:, NH:, :], gains(1, NKV), ALU.mult))
                slot = 1 - par2
                v.wait_ge(rope_ld[slot], half * 16 + 16)
                v.tensor_tensor(rope_a[:], xn[:], rope_t[:, slot, 0, :].unsqueeze(1).broadcast_to([P, NH + NKV, HD]), ALU.mult)
                pairs = "p h (e two) -> p h e two"
                for two in range(2):
                    o = v.tensor_tensor(rope_b[:].rearrange(pairs, two=2)[:, :, :, two], xn[:].rearrange(pairs, two=2)[:, :, :, 1 - two],
                                        rope_t[:, slot, 1, :].rearrange("p (e two) -> p e two", two=2)[:, :, two].unsqueeze(1)
                                        .broadcast_to([P, NH + NKV, HD // 2]), ALU.mult)
                chain(o)
                v.tensor_tensor(heads(q_lat[:, bass.ds(tile - 1, 1), :].rearrange("p a n -> p (a n)")), rope_a[:, 0:NH, :], rope_b[:, 0:NH, :], ALU.add)
                v.tensor_tensor(xk[:], rope_a[:, NH:, :], rope_b[:, NH:, :], ALU.add).then_inc(k_rdy, 1)
                k_lo_of(tile + 1, xk[:])

            v.wait_ge(past_ld, 32)
            qkv_tile(0, 0, True)
            with v.Fori(0, NQ // 2) as i:
                chain.enter(i, 8)
                for j in range(2):
                    qkv_tile(i * 2 + (j + 1), 1 - j, False, i)
            chain.leave(NQ // 2)

            def qs_split(tile, j):
                v.wait_ge(qs_hi, tile.unit0 + (j + 1))
                kv = j % 2
                if tile.ctx:
                    src = q_ctx[:, kv * G:(kv + 1) * G, :]
                else:
                    src = q_lat[:, bass.ds(tile.q + j // 2, 1), kv * 256:(kv + 1) * 256].rearrange("p a (h d) -> p (a h) d", h=G)
                lo(qs[:, :, 1, 0, :].bitcast(F32R), src, qs[:, :, 0, 0, :])
                lo(qs[:, :, 1, 1, :].bitcast(F32R), src, qs[:, :, 0, 1, :]).then_inc(qs_lo, 1)

            def step(tile, s):
                if has_score(tile, s):
                    h = s + 1
                    nb, nw = (3, CH) if tile.nk > 1 else (1, P)
                    b0 = 3 * (h % 2)
                    v.wait_ge(s_done, tile.head0 + (h + 1))
                    v.tensor_reduce(small[:, h % 4:h % 4 + 1], ps[:, b0:b0 + nb, 0:nw], mybir.AxisListType.XY, ALU.max, negate=True).then_inc(mx_done, 1)
                if has_trans(s):
                    h = s - 1
                    nb = min(3, tile.nk)
                    for r in range(tile.rounds):
                        bank = tile.loc(("t", h, r)) % 2
                        v.wait_ge(th_hi, tile.round0 + (tile.rounds * h + r + 1))
                        lo(pt[:, 1, 3 * r:3 * r + nb, h % 4, :], ps[:, 6 + bank, 0:nb * P].rearrange("p (b t) -> p b t", b=nb),
                           pt[:, 0, 3 * r:3 * r + nb, h % 4, :]).then_inc(t_free[bank], 1)
                if has_trans(s) and (s - 1) % 4 == 3:
                    j = (s - 1) // 4
                    bank = tile.loc(("o", j, 0)) % 2
                    v.wait_ge(o_cp, tile.unit0 + (j + 1))
                    for odd, done in ((0, o_sum), (1, t_free[bank])):
                        v.tensor_tensor(o_f[HD * odd:HD * odd + HD, :, :],
                                        ps[0:HD, 6 + bank, :].rearrange("p (a h t) -> p a h t", h=2, t=P)[:, :, odd, :],
                                        o_t[0:HD, :, :].rearrange("p (a h) t -> p a h t", h=2)[:, :, odd, :], ALU.add).then_inc(done, 1)
                    v.wait_ge(m_hi, tile.unit0 + (j + 1))
                    tk = 0 if tile.ctx else tile.q + 1
                    lo(act_b[:, 2 * j:2 * j + 2, 1, bass.ds(tk * P, P)], o_f[:], act_b[:, 2 * j:2 * j + 2, 0, bass.ds(tk * P, P)]).then_inc(m_att, 1)
                if has_score(tile, s):
                    h = s + 1
                    v.wait_ge(exp_done, tile.head0 + (h + 1))
                    v.reciprocal(small[:, 16 + h % 4:17 + h % 4], small[:, 8 + h % 4:9 + h % 4]).then_inc(rinv_done, 1)
                if rounds_queries(tile, s):
                    qs_split(tile, s // 4 + 1)

            att_steps(v, step, lambda tile: qs_split(tile, 0))

            for g in range(NPG):
                v.wait_ge(ph_hi, g + 1)
                for start, u0, n in ((8, 0, CTX), (CTX + 16, CTX, LAT)):
                    o = lo(ph[:, g, 1, u0:u0 + n], pp[:, g, start:start + n], ph[:, g, 0, u0:u0 + n])
                o.then_inc(ph_lo, 1)
            flat = "p g d -> p (g d)"
            d_lo_at(D_WPOOL, D_WPOOL % 2, wp[:, 1, :, :].rearrange(flat), wp[:, 0, :, :].rearrange(flat), NPG * P)

            def wo_lo(l, k, d0):
                d_lo_at(d0 + k, (d0 + k) % 2, wo[l][:, k, 1, :], wo[l][:, k, 0, :])

            for g in range(NPG):
                wo_lo(0, g, D_OUT0)
                v.wait_ge(mix_hi, g + 1)
                lo(act_b[:, 4 + g, 1, :], mf[:], act_b[:, 4 + g, 0, :]).then_inc(mix_lo, 1)
            for k in range(4, KD):
                wo_lo(0, k, D_OUT0)

            def conv3(dst, line, w, done):
                n = PADW - 3
                chain(v.tensor_scalar(dst[:, 1:1 + n], line[:, 0:n], w(0), w(3), ALU.mult, ALU.add))
                chain(v.scalar_tensor_tensor(dst[:, 1:1 + n], line[:, 1:1 + n], w(1), dst[:, 1:1 + n], ALU.mult, ALU.add))
                o = v.scalar_tensor_tensor(dst[:, 1:1 + n], line[:, 2:2 + n], w(2), dst[:, 1:1 + n], ALU.mult, ALU.add)
                if done is None:
                    chain(o)
                else:
                    o.then_inc(done, 1)

            class Ffn:
                def __init__(self, l, u0, d0):
                    self.l, self.u0, self.d0 = l, u0, d0

                def lo_u(self, g, j):
                    u_lo_at(g * 4 + (self.u0 + j), None, j % 2)

                def body(self, g, last):
                    l, u0, d0 = self.l, self.u0, self.d0
                    taps = par[:, 88 * l:88 * l + 88].rearrange("p (j f) -> p j f", j=4)
                    chain(v.tensor_copy(fgrp[:], taps[:, :, bass.ds(g * 2, 2)]))
                    for b in range(2):
                        q = g * 2 + (NF * l + b)
                        self.lo_u(g, 2 * b + 1)
                        r = 2 + (NF + 1) * l + b
                        v.wait_ge(bank_free[0], g * 6 + (3 * r + 6))
                        v.wait_ge(silu_done, q + 1)
                        conv3(f_t[l], f_a, lambda j: fgrp[:, j, b:b + 1], conv_done)
                        if b == 0:
                            self.lo_u(g, 2)
                            for j in range(2):
                                d_lo_at(d0 + j, (d0 + j) % 2, dw[:, j, 1, :], dw[:, j, 0, :], g=g)
                        elif not last:
                            self.lo_u(g + 1, 0)
                        v.wait_ge(silu_done, q + 2)

                        def mult(c):
                            v.wait_ge(up_done, g * 12 + (6 + 3 * (u0 + 2 * b + 1) + c + 1))
                            for s0, ln, p0 in PIECES[c]:
                                o = v.tensor_tensor(f_h[l][:, s0:s0 + ln], f_s[l][:, p0:p0 + ln], ps[:, 3 + c, s0 - c * CH:s0 - c * CH + ln], ALU.mult)
                            o.then_inc(h_mul, 1)

                        def h_split(c):
                            v.wait_ge(h_hi, q * 3 + (c + 1))
                            sl = slice(c * CH, (c + 1) * CH)
                            lo(hh[l][:, b, 1, sl], f_h[l][:, sl], hh[l][:, b, 0, sl]).then_inc(h_rdy, 1)

                        mult(0)
                        mult(1)
                        h_split(0)
                        mult(2)
                        h_split(1)
                        h_split(2)
                    if isinstance(g, int) and g == 0:
                        v.wait_ge(acc_zero, l + 1)
                    for j in range(2 * NT):
                        a = acc[l][:, j // 2, 512 * (j % 2):512 * (j % 2) + 512]
                        v.wait_ge(down_done, g * 18 + (18 * NG * l + j + 1))
                        v.tensor_tensor(a, a, ps[:, 6 + j % 2, :], ALU.add).then_inc(down_added, 1)

                def run(self):
                    self.body(0, False)
                    with v.Fori(0, NG - 2) as i:
                        chain.enter(i, 5)
                        self.body(i + 1, False)
                    chain.leave(NG - 2)
                    self.body(NG - 1, True)

            f = Ffn(0, U_FFN0, D_DOWN0)
            f.lo_u(0, 0)
            ln_vec("mid0", act_b, from_psum)
            f.run()
            u_lo_at(U_FOUR, None, 0)
            ln_vec("end0", act_b, from_acc(0))

            d_lo_at(D_CHAN, D_CHAN % 2, chan[:, 1, :], chan[:, 0, :], 2 * P)
            u_lo_at(U_FOUR + 1, None, 1)
            for b in range(FB):
                if b:
                    u_lo_at(U_CONV, None, 0)
                for c in range(NCH):
                    v.wait_ge(fi_hi, 3 * b + c + 1)
                    sl = slice(c * CH, (c + 1) * CH)
                    lo(f_in[:, b, 1, sl], ps[:, 3 * b + c, 0:CH], f_in[:, b, 0, sl]).then_inc(bank_free[b], 1)
            cols_of(range(6, 8))
            d_lo_at(D_CTAB, D_CTAB % 2, dw[:, 0, 1, 0:2 * P], dw[:, 0, 0, 0:2 * P], 2 * P)
            for tile in range(NT):
                v.wait_ge(fc_hi, tile + 1)
                lo(f_ch[:, tile, 1, :], ps[:, 6 + tile % 2, :], f_ch[:, tile, 0, :]).then_inc(fc_lo, 1)
            for k in range(16):
                s = (k + 1) % 2
                d_lo_at(D_TAB + k, (D_TAB + k) % 2, dw[:, s, 1, :], dw[:, s, 0, :])
            for b in range(FB):
                for h in range(3):
                    v.wait_ge(pos_hi, 3 * b + h + 1)
                    sl = slice(0, CTX) if h == 0 else slice(CTX + 512 * (h - 1), CTX + 512 * h)
                    i = ps[:, 4 + b, 0:P] if h == 0 else ps[:, 2 * b + h - 1, :]
                    lo(act_a[:, CB + b, 1, sl], i, act_a[:, CB + b, 0, sl]).then_inc(pos_lo, 1)

            v.wait_ge(pads, 2)
            taps6 = par[:, 176:200].rearrange("p (j f) -> p j f", j=4)
            with v.Fori(0, CB // 2) as i:
                chain.enter(i, 7)
                chain(v.tensor_copy(fgrp[:], taps6[:, :, bass.ds(i * 2, 2)]))
                for j in range(2):
                    b = i * 2 + j
                    u_lo_at(*conv_unit(i, 3 * j + 1))
                    u_lo_at(*conv_unit(i, 3 * j + 2))
                    n = conv_unit(i, 3 * j + 1)[0]
                    b0 = 3 * ((3 * j + 1) % 2)
                    for c in range(NCH):
                        v.wait_ge(ch_rdy, b * 3 + (c + 1))
                        v.wait_ge(up_done, n * 3 + (6 + c + 1))
                        for s0, ln, p0 in PIECES[c]:
                            o = v.tensor_tensor(c_p[:, p0:p0 + ln], c_h[:, s0:s0 + ln], ps[:, b0 + c, s0 - c * CH:s0 - c * CH + ln], ALU.mult)
                        o.then_inc(cp_rdy, 1)
                    v.wait_ge(cp_rdy, b * 3 + 6)
                    conv3(c_t, c_p, lambda k: fgrp[:, k, j:j + 1], None)
                    u_lo_at(*conv_unit(i, 3 * j + 3))
                    n = conv_unit(i, 3 * j + 2)[0]
                    b0 = 3 * ((3 * j + 2) % 2)
                    for c in range(NCH):
                        v.wait_ge(up_done, n * 3 + (6 + c + 1))
                        for s0, ln, p0 in PIECES[c]:
                            o = v.tensor_tensor(c_m[:, s0:s0 + ln], c_t[:, p0:p0 + ln], ps[:, b0 + c, s0 - c * CH:s0 - c * CH + ln], ALU.mult)
                        o.then_inc(cm_rdy, 1)
                    for c in range(NCH):
                        v.wait_ge(cm_hi, b * 3 + (c + 1))
                        sl = slice(c * CH, (c + 1) * CH)
                        line = "p a n -> p (a n)"
                        lo(act_a[:, bass.ds(b, 1), 1, sl].rearrange(line), c_m[:, sl], act_a[:, bass.ds(b, 1), 0, sl].rearrange(line)).then_inc(cm_lo, 1)
            chain.leave(CB // 2)
            for k in range(KD):
                wo_lo(1, k, D_OUT1)
            ln_vec("mid1", act_a, from_psum)
            Ffn(1, U_FFN1, D_DOWN1).run()
            ln_vec("end1", None, from_acc(1))

        @block.tensor
        def _(pe):
            PASSES = ((0, 0), (0, 1), (1, 0))

            pe.wait_ge(s_con, 16 * 10)
            for o, rows, i in ((0, 88, 0), (88, 88, 1), (176, 28, 2), (204, 16, 3)):
                pe.transpose(ps[:, 0, o:o + rows], prow[0:rows, i, :], ident[0:rows, 0:rows]).then_inc(setup_t, 1)

            def ada_block(m):
                n = 4 * m if m < 16 else D_ADA1 + 4 * (m - 16)
                pe.wait_ge(ada_bank, m + 1)
                for u in range(4):
                    pe.wait_ge(d_loaded[(n + u) % 2], 16 * ((n + u) // 2 + 1))
                    for kk in range(2):
                        mm = pe.matmul(ps[0:2, m % 3, :], conds[:, 2 * u + kk, :], raw_d[:, (n + u) % 2, kk * 512:(kk + 1) * 512],
                                       start=(u, kk) == (0, 0), stop=(u, kk) == (3, 1))
                    mm.then_inc(d_split, 1)

            def cols_mm(ns):
                for n in ns:
                    pe.wait_ge(brow[n % 2], 32 * (n // 2 + 1))
                    if n >= 2:
                        pe.wait_ge(cols_done, n - 1)
                    for k in range(KD):
                        mm = pe.matmul(ps[:, 6 + n % 2, 2 * k:2 * k + 2], bias_row[n % 2][0:3, k * P:(k + 1) * P], con[0:3, C_SELC:C_SELC + 2],
                                       start=True, stop=True)
                    mm.then_inc(brow_mm, 1)

            pe.wait_ge(setup_c, 2)
            for m in range(4):
                ada_block(m)
            cols_mm(range(2))

            def gate(cond, i1):
                for h in range(2):
                    mm = pe.matmul(ps[:, 6 + h, :], con[0:3, C_SELB + P * cond:C_SELB + P * (cond + 1)], ln_u[0:3, 512 * h:512 * (h + 1)],
                                   start=True, stop=True)
                mm.then_inc(gate_mm, 1)

            def ln_turn(tile, i4):
                pe.wait_ge(z_rdy, NT * i4 + tile + 1)
                if tile:
                    pe.wait_ge(mod_done, NT * i4 + tile)
                for k in range(KD):
                    mm = pe.transpose(ps[:, 6 + k // 4, (k % 4) * P:(k % 4 + 1) * P], ln_z[:, k * P:(k + 1) * P], ident)
                mm.then_inc(zt_done, 1)

            def gates(i1):
                pe.wait_ge(gate_ld, 32 * (i1 + 1))
                gate(1, i1)
                pe.wait_ge(gate_rdy, 2 * i1 + 1)
                gate(0, i1)

            def ln_mid(l, kind, src):
                i1, i4 = LN[kind]["i1"], LN[kind]["i4"]

                def project(tile):
                    if tile >= 3:
                        pe.wait_ge(out_evac, NT * i1 + tile - 2)
                    for h in range(2):
                        for k in range(KD):
                            for a, w in PASSES:
                                mm = pe.matmul(ps[:, 2 * (tile % 3) + h, :], src[:, k, a, tile * P:(tile + 1) * P], wo[l][:, k, w, 512 * h:512 * (h + 1)],
                                               start=(k, a, w) == (0, 0, 0), stop=(k, a, w) == (KD - 1, 1, 0))
                    mm.then_inc(out_done, 1)

                project(0)
                gates(i1)
                project(1)
                project(2)
                pe.wait_ge(gate_rdy, 2 * i1 + 2)
                for tile in range(NT):
                    ln_turn(tile, i4)
                    if tile + 3 < NT:
                        project(tile + 3)

            def chunk(out, u_slot, src, c):
                for k in range(KD):
                    for w, a in PASSES:
                        mm = pe.matmul(out, uw[:, u_slot, w, k, :], src[:, k, a, c * CH:(c + 1) * CH],
                                       start=(k, w, a) == (0, 0, 0), stop=(k, w, a) == (KD - 1, 1, 0))
                mm.then_inc(up_done, 1)

            def ln_turns(kind):
                for s in range(NT + 1):
                    for m in ada_steps(kind).get(s, []):
                        ada_block(m)
                    if s:
                        ln_turn(s - 1, LN[kind]["i4"])

            pe.wait_ge(cols_done, 2)
            ln_turns("in")
            pe.wait_ge(ada_bank, 3 + 16)
            for n in range(U_POOL, U_FFN0):
                pe.wait_ge(u_split, n + 3)
                for c in range(NCH):
                    if n == 0:
                        pe.wait_ge(act_rdy, 3 * (c + 1))
                    pe.wait_ge(bank_free[n % 2], 3 * (n // 2) + c + 1)
                    chunk(ps[:, 3 * (n % 2) + c, 0:CH], n % 2, act_a, c)

            pe.wait_ge(act_rdy, NT)
            cols_mm(range(2, 6))
            pe.wait_ge(bank_free[0], 9)
            pe.wait_ge(bank_free[1], 9)
            pe.wait_ge(d_split, D_WPOOL + 2)

            def qkv(tile):
                par2 = tile % 2
                if tile >= 2:
                    pe.wait_ge(qkv_free, tile - 1)
                for k in range(KD):
                    for a, w in PASSES:
                        x = act_a[:, k, a, tile * P:(tile + 1) * P]
                        st, sp_ = (k, a, w) == (0, 0, 0), (k, a, w) == (KD - 1, 1, 0)
                        pe.matmul(ps[:, 2 * par2, :], x, wq[:, k, w, :], start=st, stop=sp_)
                        mm = pe.matmul(ps[:, 2 * par2 + 1, 0:256], x, wkv[:, k, w, :], start=st, stop=sp_)
                mm.then_inc(qkv_done, 1)

            def turn_keys(idx):
                pe.wait_ge(k_lo, idx + 1)
                if idx >= 2:
                    pe.wait_ge(kt_ev, idx - 1)
                for kv in range(NKV):
                    mm = pe.transpose(ps[:, 4 + idx % 2, kv * P:(kv + 1) * P], k4[:, kv, :, :].rearrange("p a d -> p (a d)"), ident)
                mm.then_inc(kt_tr, 1)

            qkv(0)
            qkv(1)
            turn_keys(0)
            turn_keys(1)
            for tile in range(2, NT):
                qkv(tile)
                turn_keys(tile)
            turn_keys(NT)

            def turn_queries(tile, j):
                pe.wait_ge(qs_lo, tile.unit0 + (j + 1))
                for r in range(2):
                    loc = tile.loc(("q", j, r))
                    tile.wait_bank(pe, loc)
                    for h in range(2):
                        for a in range(2):
                            mm = pe.transpose(ps[:, 6 + loc % 2, (2 * h + a) * P:(2 * h + a + 1) * P],
                                              qs[:, 2 * r + h, a, :, :].rearrange("p b d -> p (b d)"), ident)
                mm.then_inc(qt_tr, 1)

            def first(tile):
                if tile.ctx:
                    pe.wait_ge(qkv_free, NT)
                    pe.wait_ge(kt_ev, NT + 1)
                turn_queries(tile, 0)

            def step(tile, s):
                if turns_queries(tile, s):
                    turn_queries(tile, (s - 1) // 4 + 1)
                if has_score(tile, s):
                    h = s + 1
                    j = h // 4
                    if h % 4 == 0:
                        for r in range(2):
                            tile.wait_evac(pe, tile.loc(("q", j, r)))
                    if tile.ctx:
                        if h >= 2:
                            pe.wait_ge(exp_done, h - 1)
                    else:
                        pe.wait_ge(exp_done, tile.head0 + (h - 1))
                    for c in range(3 if tile.nk > 1 else 1):
                        nw = CH if tile.nk > 1 else P
                        k0 = tile.key0 + c * CH
                        for a in range(2):
                            mm = pe.matmul(ps[:, 3 * (h % 2) + c, 0:nw], qt[:, j % 2, h % 4, a, :], kt[:, j % 2, k0:k0 + nw],
                                           start=a == 0, stop=a == 1)
                    mm.then_inc(s_done, 1)
                if has_trans(s):
                    h = s - 1
                    pe.wait_ge(p_rdy, tile.head0 + (h + 1))
                    for r in range(tile.rounds):
                        loc = tile.loc(("t", h, r))
                        tile.wait_bank(pe, loc)
                        for b in range(min(3, tile.nk)):
                            mm = pe.transpose(ps[:, 6 + loc % 2, b * P:(b + 1) * P], prob[:, h % 4, (3 * r + b) * P:(3 * r + b + 1) * P], ident)
                        mm.then_inc(tr_done, 1)
                    if h % 4 == 3:
                        j = h // 4
                        loc = tile.loc(("o", j, 0))
                        tile.wait_bank(pe, loc)
                        tile.wait_evac(pe, loc - 1)
                        for a in range(2):
                            for kb in range(tile.nk):
                                mm = pe.matmul(ps[:, 6 + loc % 2, :], vhl[:, tile.key0 // P + kb, j, :, :].rearrange("p a d -> p (a d)"),
                                               pt[:, a, kb, :, :].rearrange("p h t -> p (h t)"),
                                               start=(a, kb) == (0, 0), stop=(a, kb) == (1, tile.nk - 1))
                        mm.then_inc(pv_done, 1)

            att_steps(pe, step, first)

            pe.wait_ge(d_split, D_WPOOL + 3)
            for g in range(NPG):
                pe.wait_ge(ph_lo, g + 1)
                if g >= 2:
                    pe.wait_ge(mix_ev, g - 1)
                for c in range(NCH):
                    for w, a in PASSES:
                        mm = pe.matmul(ps[:, 3 * (g % 2) + c, 0:CH], wp[:, w, g, :], ph[:, g, a, c * CH:(c + 1) * CH],
                                       start=(w, a) == (0, 0), stop=(w, a) == (1, 0))
                mm.then_inc(mix_done, 1)

            def up_units(g, l, u0):
                for b in range(2):
                    for gate_unit in range(2):
                        pe.wait_ge(u_split, g * 4 + (u0 + 2 * b + gate_unit + 3))
                        for c in range(NCH):
                            if b == 0 and gate_unit == 0:
                                pe.wait_ge(act_rdy, NT * (2 * l + 1) + 3 * (c + 1))
                            if gate_unit:
                                pe.wait_ge(h_mul, g * 6 + (66 * l + 3 * b + c + 1))
                            else:
                                r = 2 + (NF + 1) * l + b
                                pe.wait_ge(bank_free[0], g * 6 + (3 * r + c + 1))
                            chunk(ps[:, 3 * gate_unit + c, 0:CH], gate_unit, act_b if l == 0 else act_a, c)

            def ffn(l, u0, d0):
                with pe.Fori(0, NG) as g:
                    up_units(g, l, u0)
                    pe.wait_ge(d_split, g * 2 + (d0 + 4))
                    for j in range(2 * NT):
                        tile, h = j // 2, j % 2
                        if h == 0 and tile % 3 == 0:
                            pe.wait_ge(h_rdy, g * 6 + (66 * l + 3 + tile // 3 + 1))
                        pe.wait_ge(down_added, g * 18 + (18 * NG * l + j + 1))
                        for b in range(2):
                            for a, w in PASSES:
                                mm = pe.matmul(ps[:, 6 + h, :], hh[l][:, b, a, tile * P:(tile + 1) * P], dw[:, b, w, 512 * h:512 * (h + 1)],
                                               start=(b, a, w) == (0, 0, 0), stop=(b, a, w) == (1, 1, 0))
                        mm.then_inc(down_done, 1)

            def ln_end(kind):
                i1, i4 = LN[kind]["i1"], LN[kind]["i4"]
                pe.wait_ge(down_added, 2 + 18 * NG * ((i1 + 1) // 2))
                gates(i1)
                if i4 is not None:
                    pe.wait_ge(gate_rdy, 2 * i1 + 2)
                    ln_turns(kind)

            pe.wait_ge(d_split, D_OUT0 + KD + 2)
            pe.wait_ge(mix_lo, NPG)
            pe.wait_ge(m_att, 2 + 2 * NQ)
            ln_mid(0, "mid0", act_b)
            ffn(0, U_FFN0, D_DOWN0)
            ln_end("end0")

            pe.wait_ge(ada_bank, 3 + 24)
            for b in range(FB):
                n = U_FOUR + b
                pe.wait_ge(u_split, n + 3)
                for c in range(NCH):
                    if b == 0:
                        pe.wait_ge(act_rdy, 2 * NT + 3 * (c + 1))
                    pe.wait_ge(bank_free[b], 3 * (24, 2)[b] + c + 1)
                    chunk(ps[:, 3 * b + c, 0:CH], n % 2, act_b, c)
            pe.wait_ge(d_split, D_CHAN + 3)
            pe.wait_ge(bank_free[0], 78)
            pe.wait_ge(bank_free[1], 12)
            cols_mm(range(6, 8))
            pe.wait_ge(cols_done, 8)
            for tile in range(NT):
                if tile >= 2:
                    pe.wait_ge(fc_lo, tile - 1)
                for b in range(FB):
                    for a, w in PASSES:
                        mm = pe.matmul(ps[:, 6 + tile % 2, 2 * P * b:2 * P * (b + 1)], f_in[:, b, a, tile * P:(tile + 1) * P], chan[:, w, :],
                                       start=(a, w) == (0, 0), stop=(a, w) == (1, 0))
                mm.then_inc(fc_done, 1)

            def f_part(tile, a, b, s):
                return f_ch[:, tile, a, 2 * P * b + P * s:2 * P * b + P * (s + 1)]

            pe.wait_ge(fc_lo, NT)
            pe.wait_ge(d_split, D_CTAB + 3)
            for b in range(FB):
                for s in range(2):
                    for a, w in PASSES:
                        mm = pe.matmul(ps[:, 4 + b, 0:P], f_part(0, a, b, s), dw[:, 0, w, s * P:(s + 1) * P],
                                       start=(s, a, w) == (0, 0, 0), stop=(s, a, w) == (1, 1, 0))
            mm.then_inc(d_used, 1)
            for k in range(16):
                pe.wait_ge(d_split, D_TAB + k + 3)
                for b in range(FB):
                    for h in range(2):
                        for a, w in PASSES:
                            mm = pe.matmul(ps[:, 2 * b + h, :], f_part(1 + k // 2, a, b, k % 2), dw[:, (k + 1) % 2, w, 512 * h:512 * (h + 1)],
                                           start=k == 0 and (a, w) == (0, 0), stop=k == 15 and (a, w) == (1, 0))
                mm.then_inc(d_used, 1)

            pe.wait_ge(pos_lo, 6)
            with pe.Fori(0, CB // 2) as i:
                for e in range(6):
                    j, m = e // 3, e % 3
                    n, _h, slot = conv_unit(i, e)
                    pe.wait_ge(u_split, n + 3)
                    for c in range(NCH):
                        pe.wait_ge((cp_rdy, cm_rdy, ch_rdy)[m], i * 6 + (3 * j + c + 1))
                        chunk(ps[:, 3 * slot + c, 0:CH], slot, act_b, c)

            pe.wait_ge(d_split, D_OUT1 + KD + 2)
            pe.wait_ge(cm_lo, 3 * CB)
            ln_mid(1, "mid1", act_a)
            ffn(1, U_FFN1, D_DOWN1)
            ln_end("end1")


INS = ["cache_k", "cache_v", "c", "c_ctx", "w_ada", "b_ada", "w_in_even", "q_norm_g", "k_norm_g", "w_pool", "pool_scale",
       "w_in_odd", "conv_w", "conv_b", "w_out", "w_up", "ffn_conv_w", "ffn_conv_b", "w_down", "ln_g", "ln_b"]


def kernel(**inputs):
    import concourse.bacc as _bacc
    from concourse.bass_utils import run_bass_kernel_spmd as _run

    nc = _bacc.Bacc("TRN2", target_bir_lowering=False, num_devices=1, dynamic_dma_scratch_size=1024)
    host = {name: np.ascontiguousarray(inputs[name]) for name in INS}
    host["x_all"] = np.concatenate([np.asarray(inputs["x_prompt"])[0], np.asarray(inputs["x_sample"])[0]], 0)
    host.update(constants())
    t = {name: nc.dram_tensor(f"in_{name}", a.shape, F32, kind="ExternalInput").ap() for name, a in host.items()}
    outs = {"y_all": (TOK, D), "new_k": (1, 1, CTX, NKV, HD), "new_v": (1, 1, CTX, NKV, HD)}
    for name, shape in outs.items():
        t[name] = nc.dram_tensor(f"out_{name}", shape, F32, kind="ExternalOutput").ap()
    t["xs"] = nc.dram_tensor("xs", (3, TOK, D), F32, kind="Internal").ap()
    t["ada"] = nc.dram_tensor("ada", (2, 2, 6 * D), F32, kind="Internal").ap()
    build(nc, t)
    r = _run(nc, [{f"in_{name}": a for name, a in host.items()}], core_ids=[0]).results[0]
    y = r["out_y_all"]
    return (y[:CTX].reshape(1, CTX, D), y[CTX:].reshape(1, LAT, D), r["out_new_k"], r["out_new_v"])
```

```python
from contextlib import ExitStack

import numpy as np

import concourse.bass as bass
from concourse import mybir

F32 = mybir.dt.float32
F32R = mybir.dt.float32r
ALU = mybir.AluOpType
ACT = mybir.ActivationFunctionType
AX_X = mybir.AxisListType.X

P = 128
D = 1024
KD = D // P
CTX, LAT, PAST = 128, 1024, 128
TOK = CTX + LAT
NT = TOK // P
NQ = LAT // P
CH = 384
NCH = TOK // CH
HD, NH, NKV = 64, 8, 2
G = NH // NKV
AW = NH * HD
QK = AW + NKV * HD
IN_E = AW + 2 * NKV * HD + (D - AW)
NPG = 4
WINDOWS = (2, 4, 8, 16)
CW = 768
CB = CW // P
FW = D - CW
FB = FW // P
DFF = 2816
NF = DFF // P
NG = NF // 2
ALPHA = 4.0 ** 0.25
EPS = 1e-6
PADW = TOK + 4
PIECES = [[(0, CTX, 1), (CTX, CH - CTX, CTX + 2)]] + [[(c * CH, CH, c * CH + 2)] for c in range(1, NCH)]
PPW = TOK + 24
PPIECES = [[(0, CTX, 8), (CTX, CH - CTX, CTX + 16)]] + [[(c * CH, CH, c * CH + 16)] for c in range(1, NCH)]
NKEY = LAT + PAST + CTX
LKB = (LAT + PAST) // P

U_POOL, U_FFN0, U_FOUR, U_CONV, U_FFN1 = 0, 4, 4 + 4 * NG, 6 + 4 * NG, 24 + 4 * NG
D_QKV = 0
D_WPOOL = D_QKV + KD + KD // 2
D_OUT0 = D_WPOOL + 1
D_DOWN0 = D_OUT0 + 4
D_CHAN = D_DOWN0 + NF
D_CTAB = D_CHAN + 1
D_TAB = D_CTAB + 1
D_OUT1 = D_TAB + 16
D_DOWN1 = D_OUT1 + 4
OUT_EXTRA = range(2, 6)
ADA_SLOTS = 6
CHUNKS = (0, 1, 3, 4)


def ada_half(m):
    if m < 6:
        return 0, m
    if m < 10:
        return 1, m - 6
    return (0, m - 4) if m < 16 else (1, m - 12)


def ada_steps(kind):
    if kind == "in":
        return {s: [4 + 2 * s, 5 + 2 * s] if s < 3 else [7 + s] for s in range(9)}
    return {s: [15 + s] for s in range(1, 9)} if kind == "end0" else {}



C_ID, C_EDGE, C_SELC, C_SELB, C_EPS, NCON = 0, 128, 192, 194, 450, 452


def constants():
    con = np.zeros((P, NCON), np.float32)
    con[:, C_ID:C_ID + P] = np.eye(P)
    for g, w in enumerate(WINDOWS):
        for j in range(8):
            con[:, C_EDGE + 16 * g + j] = w / (min(j + w // 2, CTX) - max(j - w // 2, 0))
            t = CTX - 8 + j
            con[:, C_EDGE + 16 * g + 8 + j] = w / (min(t + w // 2, CTX) - max(t - w // 2, 0))
    for cond in range(2):
        for r in (cond, 2):
            con[r, C_SELC + cond] = 1
            con[r, C_SELB + P * cond:C_SELB + P * (cond + 1)] = 1
    con[:, C_EPS] = EPS
    n_freq = HD // 4
    inv = 1.0 / (10000.0 ** (np.arange(n_freq) / n_freq))
    t = np.arange(LAT)
    ang = np.concatenate([(t // 64)[:, None] * inv, (t % 64)[:, None] * inv], -1)
    rope = np.zeros((LAT, 2, HD // 2, 2))
    rope[:, 0] = np.cos(ang)[:, :, None]
    rope[:, 1, :, 0], rope[:, 1, :, 1] = -np.sin(ang), np.sin(ang)
    a = 2 * np.pi * np.outer(np.arange(64), np.arange(64)) / 64
    chan = np.zeros((P, 2, P))
    for b in range(2):
        s = slice(64 * b, 64 * b + 64)
        chan[s, 0, s], chan[s, 1, s] = np.cos(a) / 8, np.sin(a) / 8

    def table(n):
        a = 2 * np.pi * (np.outer(np.arange(n), np.arange(n)) % n) / n
        return np.cos(a) / np.sqrt(n), -np.sin(a) / np.sqrt(n)

    cc, cs = table(CTX)
    lc, ls = table(LAT)
    pos = np.stack([lc.reshape(8, P, LAT), ls.reshape(8, P, LAT)], 1)
    f = np.float32
    return {"k_con": con, "k_rope": rope.reshape(LAT, 2 * HD).astype(f), "k_chan": chan.reshape(P, 2 * P).astype(f),
            "k_ctab": np.concatenate([cc, cs], 1).astype(f), "k_pos": pos.reshape(16, P, LAT).astype(f)}


def build(nc, t):
    ctx = ExitStack()
    with ctx:
        base = (nc.sbuf_base + 31) // 32 * 32
        REG = 8 * 2 * TOK * 4
        off_a, off_b = base, base + REG
        off_c = base + 2 * REG

        def at(name, shape, dt, off):
            return nc.alloc_sbuf_tensor_at(name, shape, dt, offset=off)

        def size(shape):
            n = 4
            for x in shape[1:]:
                n *= x
            return (n + 31) // 32 * 32

        end = [off_c]

        def fixed(name, shape, dt=F32):
            r = at(name, shape, dt, end[0])
            end[0] += size(shape)
            return r

        act_a = at("act_a", [P, KD, 2, TOK], F32R, off_a)
        act_b = at("act_b", [P, KD, 2, TOK], F32R, off_b)
        con = fixed("con", [P, NCON])
        cols = fixed("cols", [P, 2, 4, KD, 2])
        par = fixed("par", [P, 220])
        conds = fixed("conds", [P, KD, 2])
        fgrp = fixed("fgrp", [P, 4, 2])
        stats = fixed("stats", [P, 3, 48])
        small = fixed("small", [P, 64])
        off_raw_u = end[0]
        raw_u = fixed("raw_u", [P, 2, KD, P])
        raw_d = fixed("raw_d", [P, 2, D])
        off_uw = end[0]
        uw = fixed("uw", [P, 2, 2, KD, P], F32R)
        off_s = end[0]
        dw = at("dw", [P, 2, 2, D], F32R, off_s)
        ident = con[:, C_ID:C_ID + P]
        eps = con[:, C_EPS:C_EPS + 1]
        ln_y = at("ln_y", [P, 3, D], F32, off_s)
        ln_t = at("ln_t", [P, D], F32, off_s + 12288)
        ln_z = at("ln_z", [P, D], F32, off_s + 16384)
        ln_u = at("ln_u", [P, D], F32, off_s + 20480)
        ln_g = at("ln_g", [P, D], F32, off_s + 24576)
        ada_w = [at(f"ada_w{i}", [P, ADA_SLOTS, 2, 512], F32, o) for i, o in enumerate((off_b, off_a + 45056))]
        ada_row = at("ada_row", [P, 3, 512], F32, off_s + 28672)
        bias_row = [at(f"bias_row{i}", [P, D], F32, off_s + 20480 + 4096 * i) for i in range(2)]
        prow = at("prow", [P, 4, P], F32, off_a)
        kt = at("kt", [P, NKV, NKEY], F32R, off_s)
        vhl = at("vhl", [P, NKEY // P, NKV, 2, HD], F32R, off_s + 10240)
        q_ctx = at("q_ctx", [P, NH, HD], F32, off_s + 20480)
        k4 = at("k4", [P, NKV, 2, HD], F32, off_s + 22528)
        xn = at("xn", [P, NH + NKV, HD], F32, off_s + 23552)
        rope_a = at("rope_a", [P, NH + NKV, HD], F32, off_s + 26112)
        rope_b = at("rope_b", [P, NH + NKV, HD], F32, off_s + 28672)
        sq = at("sq", [P, NH + NKV, HD], F32, off_s + 31232)
        rope_t = at("rope_t", [P, 2, 2, HD], F32, off_s + 33792)
        kv_out = at("kv_out", [P, 2, P], F32, off_s + 34816)
        kv_past = at("kv_past", [P, 2, P], F32, off_s + 35840)
        g_row = at("g_row", [P, 2, HD], F32, off_s + 36864)
        pool_t2 = at("pool_t2", [P, PPW], F32, off_s + 37376)
        pool_t1 = at("pool_t1", [P, PPW], F32, off_raw_u)
        xk = at("xk", [P, NKV, HD], F32, off_s + 42112)
        wp = at("wp", [P, 2, NPG, P], F32R, off_s + 24576)
        mf = at("mf", [P, TOK], F32, off_s + 28672)
        wq = at("wq", [P, KD, 2, AW], F32R, off_b)
        wkv = at("wkv", [P, KD, 2, 2 * NKV * HD], F32R, off_uw)
        pp = at("pp", [P, NPG, PPW], F32, off_b + 36864)
        q_lat = at("q_lat", [P, NQ, AW], F32, off_b + 36864 + 18816)
        pt = at("pt", [P, 2, LKB, G, P], F32R, off_a)
        prob = at("prob", [P, 4, LAT + PAST], F32, off_a + 36864)
        qs = at("qs", [P, G, 2, 2, HD], F32, off_a + 55296)
        qt = at("qt", [P, 2, G, 2, P], F32R, off_a + 59392)
        o_t = at("o_t", [P, G, P], F32, off_a + 67584)
        o_f = at("o_f", [P, 2, P], F32, off_a + 69632)
        ph = at("ph", [P, NPG, 2, TOK], F32R, off_a + 36864)
        out_raw = [at(f"out_raw{l}", [P, len(OUT_EXTRA), D], F32, o) for l, o in enumerate((off_uw, off_s))]
        wo = [at(f"wo{l}", [P, KD, 2, D], F32R, o) for l, o in enumerate((off_a, off_b))]
        gb_mid = [at(f"gbm{l}", [P, 2, D], F32, o + 65536) for l, o in enumerate((off_a, off_b))]
        gb_end = [at(f"gbe{l}", [P, 2, D], F32, o + 36864) for l, o in enumerate((off_a, off_b))]
        acc = [at(f"acc{l}", [P, NT, D], F32, o) for l, o in enumerate((off_a, off_b))]
        hh = [at(f"hh{l}", [P, 2, 2, TOK], F32R, o + 36864) for l, o in enumerate((off_a, off_b))]
        f_t = [at(f"ft{l}", [P, PADW], F32, o + 55296) for l, o in enumerate((off_a, off_b))]
        f_s = [at(f"fs{l}", [P, PADW], F32, o + 55296 + 4640) for l, o in enumerate((off_a, off_b))]
        f_h = [at(f"fh{l}", [P, PADW], F32, o + 55296 + 9280) for l, o in enumerate((off_a, off_b))]
        f_a = at("fa", [P, PADW], F32, off_s + 16384)
        f_in = at("f_in", [P, FB, 2, TOK], F32R, off_a)
        f_ch = at("f_ch", [P, NT, 2, 2 * FW], F32R, off_a + 18432)
        chan = at("chan", [P, 2, 2 * P], F32R, off_s + 16384)
        c_h = at("c_h", [P, TOK], F32, off_s + 16384 + 2048)
        c_p = at("c_p", [P, PADW], F32, off_s + 16384 + 2048 + 4608)
        c_t = at("c_t", [P, PADW], F32, off_s + 16384 + 2048 + 9248)
        c_m = at("c_m", [P, TOK], F32, off_s + 16384 + 2048 + 13888)

        ps = ctx.enter_context(nc.psum_tensor("ps", [P, 8, 512], F32))

        sems = {}

        def sem(name):
            sems[name] = ctx.enter_context(nc.semaphore(name))
            return sems[name]

        s_con = sem("s_con")
        setup_t, setup_c = sem("setup_t"), sem("setup_c")
        u_loaded = [sem(f"u_loaded{i}") for i in range(2)]
        u_hi, u_split, up_done = sem("u_hi"), sem("u_split"), sem("up_done")
        bank_free = [sem(f"bank_free{i}") for i in range(2)]
        d_loaded = [sem(f"d_loaded{i}") for i in range(2)]
        d_hi, d_split, d_used = sem("d_hi"), sem("d_split"), sem("d_used")
        ada_ld = [sem(f"ada_ld{i}") for i in range(ADA_SLOTS)]
        ada_used, ada_bank = sem("ada_used"), sem("ada_bank")
        ada_st = [sem(f"ada_st{i}") for i in range(3)]
        brow = [sem(f"brow{i}") for i in range(2)]
        brow_mm, cols_done = sem("brow_mm"), sem("cols_done")
        x_ld = [sem(f"x_ld{i}") for i in range(3)]
        x_st = [sem(f"x_st{i}") for i in range(3)]
        gb_ld, gate_ld, gate_mm, gate_rdy = sem("gb_ld"), sem("gate_ld"), sem("gate_mm"), sem("gate_rdy")
        out_ld, out_hi, out_lo = sem("out_ld"), sem("out_hi"), sem("out_lo")
        out_done, out_evac = sem("out_done"), sem("out_evac")
        stat1, sd1, rs1, norm1, x1_rdy = (sem(x) for x in ("stat1", "sd1", "rs1", "norm1", "x1_rdy"))
        stat2, sd2, rs2, z_rdy = (sem(x) for x in ("stat2", "sd2", "rs2", "z_rdy"))
        zt_done, mod_done, act_hi, act_rdy = (sem(x) for x in ("zt_done", "mod_done", "act_hi", "act_rdy"))
        v_step, g_step = sem("v_step"), sem("g_step")
        pp_zero, pool_done = sem("pp_zero"), sem("pool_done")
        g_ld, past_ld = sem("g_ld"), sem("past_ld")
        rope_ld = [sem(f"rope_ld{i}") for i in range(2)]
        qkv_done, qkv_free = sem("qkv_done"), sem("qkv_free")
        sq_done, ss_done, qsd, k_rdy, k_hi, k_lo = (sem(x) for x in ("sq_done", "ss_done", "qsd", "k_rdy", "k_hi", "k_lo"))
        kt_tr, kt_ev, v_hi, v_out, kv_st = (sem(x) for x in ("kt_tr", "kt_ev", "v_hi", "v_out", "kv_st"))
        qs_hi, qs_lo, qt_tr = (sem(x) for x in ("qs_hi", "qs_lo", "qt_tr"))
        s_done, mx_done, exp_done, rinv_done, p_rdy = (sem(x) for x in ("s_done", "mx_done", "exp_done", "rinv_done", "p_rdy"))
        tr_done, th_hi = sem("tr_done"), sem("th_hi")
        t_free = [sem(f"t_free{i}") for i in range(2)]
        pv_done, o_cp, o_sum, m_hi, m_att = (sem(x) for x in ("pv_done", "o_cp", "o_sum", "m_hi", "m_att"))
        ph_hi, ph_lo, mix_done, mix_ev, mix_hi, mix_lo = (sem(x) for x in ("ph_hi", "ph_lo", "mix_done", "mix_ev", "mix_hi", "mix_lo"))
        pads, acc_zero = sem("pads"), sem("acc_zero")
        conv_done, silu_done, h_mul, h_hi, h_rdy = (sem(x) for x in ("conv_done", "silu_done", "h_mul", "h_hi", "h_rdy"))
        down_done, down_added = sem("down_done"), sem("down_added")
        fi_hi, fc_done, fc_hi, fc_lo, pos_hi, pos_lo = (sem(x) for x in (
            "fi_hi", "fc_done", "fc_hi", "fc_lo", "pos_hi", "pos_lo"))
        ch_rdy, cp_rdy, cm_rdy, cm_hi, cm_lo = (sem(x) for x in ("ch_rdy", "cp_rdy", "cm_rdy", "cm_hi", "cm_lo"))
        g_mul = sem("g_mul")

        CREDITS = [(u_split, 2), (up_done, 6), (bank_free[0], 3), (bank_free[1], 3), (d_split, 2), (d_used, 2),
                   (ada_used, ADA_SLOTS), (ada_bank, 3), (ada_st[0], 16), (ada_st[1], 16), (ada_st[2], 16), (conv_done, 1), (silu_done, 1), (h_mul, 3),
                   (down_added, 2), (cp_rdy, 3), (cm_rdy, 3), (t_free[0], 1), (t_free[1], 1)]

        xs = t["xs"]
        ada = t["ada"]

        w_conv = t["w_in_odd"][0].rearrange("(k p) n -> p k n", p=P)

        def dram_rows(ap, tile):
            return ap[bass.ds(tile * P, P), :]

        def u_source(n, f=None):
            if f is not None:
                l, gate = n
                w, col = t["w_up"][l], gate * DFF + f * P
            elif n < U_FFN0:
                w, col = t["w_in_even"][0], QK + NKV * HD + n * P
            elif n < U_CONV:
                w, col = t["w_in_odd"][0], 3 * CW + (n - U_FOUR) * P
            return w.rearrange("(k p) n -> p k n", p=P)[:, :, bass.ds(col, P)]

        LN = {"in": dict(ph=0, i1=None, i4=0, im=None), "mid0": dict(ph=1, i1=0, i4=1, im=0),
              "end0": dict(ph=2, i1=1, i4=2, im=None), "mid1": dict(ph=3, i1=2, i4=3, im=1),
              "end1": dict(ph=4, i1=3, i4=None, im=None)}

        def ada_stored(eng, n):
            for s in range(3):
                eng.wait_ge(ada_st[s], 16 + 16 * len(range(s, n, 3)))

        class Step:
            def __init__(self, base, i=None):
                self.base, self.i = base, i

            def tile(self, lag):
                return self.base - lag if self.i is None else self.i * 3 + (self.base - lag)

            def third(self, lag):
                return (self.base - lag) // 3 if self.i is None else self.i + (self.base - lag) // 3

            def slot(self, lag):
                return (self.base - lag) % 3

            def live(self, lag):
                return self.i is not None or 0 <= self.base - lag < NT

            def first(self, lag):
                return self.i is None and self.base == lag

        def ln_steps(eng, step, loop=lambda i: None):
            for s in range(3):
                step(Step(s))
            with eng.Fori(0, 2) as i:
                loop(i)
                for s in range(3, 6):
                    step(Step(s, i))
            loop(None)
            for s in range(9, 11):
                step(Step(s))

        class QTile:
            def __init__(self, q, first=False, last=False):
                self.q, self.first, self.last, self.ctx = q, first, last, q is None
                self.middle = not (self.ctx or first)
                self.steps = range(2, 11 if last else 10) if self.middle else range(-1, 11 if self.ctx else 10)
                self.rounds = 1 if self.ctx else 3
                self.nk = 1 if self.ctx else LKB
                self.head0 = 0 if self.ctx else q * NH + NH
                self.unit0 = 0 if self.ctx else q * 2 + 2
                self.round0 = 0 if self.ctx else q * (3 * NH) + NH
                self.key0 = LAT + PAST if self.ctx else 0
                order = [] if self.middle else [("q", 0, 0), ("q", 0, 1)]
                for s in self.steps:
                    if self.output(s) is not None:
                        order.append(("o", self.output(s), 0))
                    if has_trans(s):
                        order += [("t", s - 2, r) for r in range(self.rounds)]
                    if self.turns(s):
                        order += [("q", (s - 1) // 4 + 1, r) for r in range(2)]
                self.uses = {u: n for n, u in enumerate(order)}
                if self.ctx:
                    self.base, self.grow = 0, 0
                elif first:
                    self.base, self.grow = len(QTile(None).uses), 0
                else:
                    before, per = len(QTile(None).uses) + len(QTile(0, first=True).uses), 4 + 3 * NH + 2
                    assert per % 2 == 0 and (last or len(self.uses) == per)
                    self.base, self.grow = before - per, q * (per // 2)

            def output(self, s):
                return {6: 0, 10: 1}.get(s, -1 if s == 2 and self.middle else None)

            def turns(self, s):
                return s in (1, 5, 9) and not (s > 1 and (self.ctx or self.last))

            def splits(self, s):
                return s in (0, 4, 8) and not (s > 0 and (self.ctx or self.last))

            def at(self, use):
                if self.middle and use[:2] == ("q", 1):
                    return self.base - 2 + use[2]
                return self.base + self.uses[use]

            def bank(self, use):
                return self.at(use) % 2

            def wait_bank(self, eng, use):
                n = self.at(use)
                eng.wait_ge(t_free[n % 2], self.grow + (n // 2 + 1))

            def wait_evac(self, eng, use, back=0):
                n = self.at(use) - back
                eng.wait_ge(t_free[n % 2], self.grow + (n // 2 + 2))

        def att_steps(eng, step, first):
            for tile in (QTile(None), QTile(0, first=True)):
                first(tile)
                for s in tile.steps:
                    step(tile, s)
            with eng.Fori(1, NQ - 1) as q:
                tile = QTile(q)
                for s in tile.steps:
                    step(tile, s)
            tile = QTile(NQ - 1, last=True)
            for s in tile.steps:
                step(tile, s)

        def has_score(tile, s):
            return s + 1 < NH or not (tile.ctx or tile.last)

        def has_exp(tile, s):
            return s >= 0 and (s < NH or not (tile.ctx or tile.last))

        def has_trans(s):
            return 0 <= s - 2 < NH

        def conv_unit(i, e):
            return i * 6 + (U_CONV + e), i * 3 + (U_CONV // 2 + e // 2), e % 2

        block = ctx.enter_context(nc.Block())

        @block.sync
        def _(sp):
            sp.dma_start(con[:], t["k_con"]).then_inc(s_con, 16)
            sp.dma_start(prow[0:8, 3, :], t["c"].rearrange("a (k p) -> (a k) p", p=P)).then_inc(s_con, 16)
            sp.dma_start(prow[8:16, 3, :], t["c_ctx"].rearrange("(k p) -> k p", p=P)).then_inc(s_con, 16)
            for l in range(2):
                sp.dma_start(prow[0:66, l, :], t["ffn_conv_w"][l].rearrange("j (k p) -> (j k) p", p=P)).then_inc(s_con, 16)
                sp.dma_start(prow[66:88, l, :], t["ffn_conv_b"][l:l + 1].rearrange("a (k p) -> (a k) p", p=P)).then_inc(s_con, 16)
            sp.dma_start(prow[0:18, 2, :], t["conv_w"][0].rearrange("j (k p) -> (j k) p", p=P)).then_inc(s_con, 16)
            sp.dma_start(prow[18:24, 2, :], t["conv_b"].rearrange("a (k p) -> (a k) p", p=P)).then_inc(s_con, 16)
            sp.dma_start(prow[24:28, 2, :], t["pool_scale"].rearrange("a (k p) -> (a k) p", p=P)).then_inc(s_con, 16)

            def d_unit(n, src, width=D):
                sp.wait_ge(d_split, n + 1)
                sp.dma_start(raw_d[:, n % 2, 0:width], src).then_inc(d_loaded[n % 2], 16)

            def ada_units(m, i=None):
                l, half = ada_half(m)
                col = half * 512 if i is None else i * 1536 + half * 512
                w = t["w_ada"][l].rearrange("(u kk p) n -> u p kk n", kk=2, p=P)
                for u in range(4):
                    a = 4 * m + u
                    sp.wait_ge(ada_used, a + 1 if i is None else i * 12 + (a + 1))
                    sp.dma_start(ada_w[m >= 16][:, a % ADA_SLOTS, :, :], w[u][:, :, bass.ds(col, 512)]).then_inc(ada_ld[a % ADA_SLOTS], 16)

            def bias_rows(ns, stored):
                ada_stored(sp, stored)
                if stored > 4:
                    sp.wait_ge(act_rdy, NT if stored == 16 else 3 * NT)
                for n in ns:
                    l, j = n // 4, CHUNKS[n % 4]
                    if n >= 2:
                        sp.wait_ge(brow_mm, n - 1)
                    sp.dma_start(bias_row[n % 2][0:2, :], ada[l, :, j * D:(j + 1) * D]).then_inc(brow[n % 2], 16)
                    sp.dma_start(bias_row[n % 2][2:3, :], t["b_ada"][l:l + 1, j * D:(j + 1) * D]).then_inc(brow[n % 2], 16)

            def u_unit(n, src):
                sp.wait_ge(u_split, n + 1)
                sp.dma_start(raw_u[:, n % 2, :, :], src).then_inc(u_loaded[n % 2], 16)

            for m in range(6):
                ada_units(m)
            for n in range(2):
                u_unit(n, u_source(n))
            bias_rows(range(2), 4)

            def ln_loads(kind, src, dst=None):
                i1, i4 = LN[kind]["i1"], LN[kind]["i4"]

                def load(tile, slot):
                    sp.dma_start(ln_y[:, slot, :], dram_rows(src, tile)).then_inc(x_ld[slot], 16)

                if i1 is not None:
                    l, m = (0 if kind.endswith("0") else 1), (0 if kind.startswith("mid") else 1)
                    j = (2, 5)[m]
                    sp.dma_start(ln_u[0:2, :], ada[l, :, j * D:(j + 1) * D]).then_inc(gate_ld, 16)
                    sp.dma_start(ln_u[2:3, :], t["b_ada"][l:l + 1, j * D:(j + 1) * D]).then_inc(gate_ld, 16)
                for s in range(3):
                    load(s, s)
                if i1 is not None:
                    gb = (gb_mid, gb_end)[m][l]
                    sp.dma_start(gb[:, 0, :], t["ln_g"][l, m, :].partition_broadcast(P)).then_inc(gb_ld, 16)
                    sp.dma_start(gb[:, 1, :], t["ln_b"][l, m, :].partition_broadcast(P)).then_inc(gb_ld, 16)

                for s in range(1, 3):
                    for m in ada_steps(kind).get(s, []):
                        ada_units(m)

                def step(tile, slot, used):
                    if i1 is not None:
                        sp.wait_ge(x1_rdy, tile + (NT * i1 + 1))
                        sp.dma_start(dram_rows(dst, tile), ln_y[:, slot, :]).then_inc(x_st[slot], 16)
                    if used is not None:
                        if i4 is not None:
                            sp.wait_ge(z_rdy, tile + (NT * i4 + 1))
                        if i1 is not None:
                            sp.wait_ge(x_st[slot], used * 16 + 48 * i1)
                        load(tile + 3, slot)

                with sp.Fori(0, 2) as i:
                    for j in range(3):
                        step(i * 3 + j, j, i + 1)
                        for m in ada_steps(kind).get(3 + j, []):
                            ada_units(m, i)
                for j in range(3):
                    step(6 + j, j, None)
                if i1 is not None:
                    for j in range(3):
                        sp.wait_ge(x_st[j], 48 * (i1 + 1))

            for n in range(2, 4):
                u_unit(n, u_source(n))
            for k in range(2):
                d_unit(D_QKV + k, t["w_in_even"][0][k * P:(k + 1) * P, 0:AW], AW)
            ln_loads("in", t["x_all"])
            bias_rows(range(2, 4), 16)
            for k in range(2, KD):
                d_unit(D_QKV + k, t["w_in_even"][0][k * P:(k + 1) * P, 0:AW], AW)
                if k == 4:
                    bias_rows(range(4, 6), 16)
            for k in range(KD // 2):
                n = D_QKV + KD + k
                sp.wait_ge(d_split, n + 1)
                sp.dma_start(raw_d[:, n % 2, 0:4 * NKV * HD].rearrange("p (a n) -> p a n", a=2), t["w_in_even"][0].rearrange("(k a p) n -> k p a n", a=2, p=P)
                             [k][:, :, AW:QK + NKV * HD]).then_inc(d_loaded[n % 2], 16)
            sp.dma_start(g_row[:, 0, :], t["q_norm_g"][0].partition_broadcast(P)).then_inc(g_ld, 16)
            sp.dma_start(g_row[:, 1, :], t["k_norm_g"][0].partition_broadcast(P)).then_inc(g_ld, 16)
            sp.dma_start(kv_past[:, 0, :], t["cache_k"][0, 0].rearrange("s h d -> s (h d)")).then_inc(past_ld, 16)
            sp.dma_start(kv_past[:, 1, :], t["cache_v"][0, 0].rearrange("s h d -> s (h d)")).then_inc(past_ld, 16)
            for i in range(2):
                sp.dma_start(rope_t[:, i, :, :], t["k_rope"][i * P:(i + 1) * P].rearrange("t (a d) -> t a d", a=2)).then_inc(rope_ld[i], 16)
            sp.wait_ge(d_split, D_WPOOL + 1)
            sp.dma_start(raw_d[:, D_WPOOL % 2, 0:NPG * P].rearrange("p (g d) -> p g d", g=NPG),
                         t["w_pool"][0].rearrange("g c d -> c g d")).then_inc(d_loaded[D_WPOOL % 2], 16)
            sp.wait_ge(k_rdy, 1)
            sp.dma_start(t["new_k"][0, 0].rearrange("s h d -> s (h d)"), kv_out[:, 0, :]).then_inc(kv_st, 16)
            sp.wait_ge(v_out, 1)
            sp.dma_start(t["new_v"][0, 0].rearrange("s h d -> s (h d)"), kv_out[:, 1, :]).then_inc(kv_st, 16)
            with sp.Fori(0, NQ // 2 - 1) as i:
                for j in range(2):
                    sp.wait_ge(k_rdy, i * 2 + (j + 2))
                    sp.dma_start(rope_t[:, j, :, :], dram_rows(t["k_rope"], i * 2 + (j + 2))
                                 .rearrange("t (a d) -> t a d", a=2)).then_inc(rope_ld[j], 16)

            def out_extra(l):
                for n, k in enumerate(OUT_EXTRA):
                    sp.dma_start(out_raw[l][:, n, :], t["w_out"][l][k * P:(k + 1) * P, :]).then_inc(out_ld, 16)

            def out_units(l, d0):
                for n, k in enumerate((0, 1, 6, 7)):
                    d_unit(d0 + n, t["w_out"][l][k * P:(k + 1) * P, :])

            class FfnLoads:
                def __init__(self, l, u0, d0):
                    self.l, self.u0, self.d0 = l, u0, d0

                def u(self, g, j):
                    sp.wait_ge(u_split, g * 4 + (self.u0 + j + 1))
                    sp.dma_start(raw_u[:, j % 2, :, :], u_source((self.l, j % 2), g * 2 + j // 2)).then_inc(u_loaded[j % 2], 16)

                def dn(self, g, j):
                    sp.wait_ge(d_split, g * 2 + (self.d0 + j + 1))
                    sp.dma_start(raw_d[:, (self.d0 + j) % 2, :], dram_rows(t["w_down"][self.l], g * 2 + j)).then_inc(
                        d_loaded[(self.d0 + j) % 2], 16)

                def rest(self):
                    with sp.Fori(0, NG - 1) as g:
                        self.u(g, 2)
                        self.u(g, 3)
                        self.u(g + 1, 0)
                        self.dn(g + 1, 0)
                        self.dn(g + 1, 1)
                        self.u(g + 1, 1)
                    self.u(NG - 1, 2)
                    self.u(NG - 1, 3)

            sp.wait_ge(qkv_done, NT)
            out_extra(0)
            out_units(0, D_OUT0)
            sp.wait_ge(pool_done, 1)
            f = FfnLoads(0, U_FFN0, D_DOWN0)
            f.u(0, 0)
            f.u(0, 1)
            sp.wait_ge(mix_lo, NPG)
            ln_loads("mid0", t["x_all"], xs[0])
            f.dn(0, 0)
            f.dn(0, 1)
            f.rest()
            for n in (U_FOUR, U_FOUR + 1):
                u_unit(n, u_source(n))
            sp.wait_ge(down_done, 18 * NG)
            ln_loads("end0", xs[0], xs[1])
            d_unit(D_CHAN, t["k_chan"], 2 * P)
            d_unit(D_CTAB, t["k_ctab"], 2 * P)
            bias_rows(range(6, 8), 24)
            u_unit(U_CONV, w_conv[:, :, 0:P])
            for k in range(16):
                d_unit(D_TAB + k, t["k_pos"][k])
            with sp.Fori(0, CB // 2 - 1) as i:
                for e in range(1, 7):
                    n, _h, slot = conv_unit(i, e)
                    sp.wait_ge(u_split, n + 1)
                    sp.dma_start(raw_u[:, slot, :, :], w_conv[:, :, bass.ds(i * (2 * P) + ((0, 2 * CW, CW)[e % 3] + e // 3 * P), P)]).then_inc(u_loaded[slot], 16)
            sp.wait_ge(d_used, 2 + 17)
            out_extra(1)
            for e in range(1, 6):
                n = U_CONV + 6 * (CB // 2 - 1) + e
                col = (0, 2 * CW, CW)[e % 3] + (CB - 2 + e // 3) * P
                u_unit(n, w_conv[:, :, col:col + P])
            f = FfnLoads(1, U_FFN1, D_DOWN1)
            f.u(0, 0)
            f.u(0, 1)
            out_units(1, D_OUT1)
            sp.wait_ge(out_lo, 8)
            ln_loads("mid1", xs[1], xs[2])
            f.dn(0, 0)
            f.dn(0, 1)
            f.rest()
            sp.wait_ge(down_done, 36 * NG)
            ln_loads("end1", xs[2], t["y_all"])
            sp.wait_ge(kv_st, 32)

        @block.gpsimd
        def _(gp):
            for s, v in CREDITS:
                gp.sem_inc(s, v)
            gp.memset(pp[:], 0.0).then_inc(pp_zero, 1)
            chained = [0]

            def chain(ins):
                chained[0] += 1
                ins.then_inc(g_step, 1)
                gp.wait_ge(g_step, chained[0])

            gp.wait_ge(bank_free[0], 3 + 6)
            gp.wait_ge(bank_free[1], 3 + 6)
            for g, w in enumerate(WINDOWS):
                bufs, i, width, first, last = (pool_t1, pool_t2), 0, 2, 1, PPW
                chain(gp.tensor_tensor(bufs[0][:, 1:PPW], pp[:, g, 0:PPW - 1], pp[:, g, 1:PPW], ALU.add))
                while width < w:
                    h = width // 2
                    cur, nxt = bufs[i % 2], bufs[(i + 1) % 2]
                    first, last = first + h, last - h
                    chain(gp.tensor_tensor(nxt[:, first:last], cur[:, first - h:last - h], cur[:, first + h:last + h], ALU.add))
                    width, i = width * 2, i + 1
                cur, nxt = bufs[i % 2], bufs[(i + 1) % 2]
                for start, n in ((8, CTX), (CTX + 16, LAT)):
                    for j, e in ((0, 0), (n - 8, 8)):
                        c = cur[:, start + j:start + j + 8]
                        chain(gp.tensor_tensor(c, c, con[:, C_EDGE + 16 * g + e:C_EDGE + 16 * g + e + 8], ALU.mult))
                for j, (start, n) in enumerate(((8, CTX), (CTX + 16, LAT))):
                    chain(gp.tensor_scalar(nxt[:, start:start + n], cur[:, start:start + n], 1.0 / w, 0.0, ALU.mult, ALU.add))
                    o = gp.tensor_tensor(pp[:, g, start:start + n], nxt[:, start:start + n], pp[:, g, start:start + n], ALU.subtract)
                    if g == NPG - 1 and j == 1:
                        o.then_inc(pool_done, 1)
                    else:
                        chain(o)

            def step(tile, s):
                if has_exp(tile, s):
                    h = s
                    i = tile.head0 + h
                    gp.wait_ge(rinv_done, i + 1)
                    sl = prob[:, h % 4, 0:tile.nk * P]
                    gp.tensor_tensor(sl, sl, small[:, 16 + h % 4:17 + h % 4].broadcast_to([P, tile.nk * P]), ALU.mult).then_inc(p_rdy, 1)

            att_steps(gp, step, lambda tile: None)

            def out_split():
                for n, k in enumerate(OUT_EXTRA):
                    gp.wait_ge(out_hi, n + 1)
                    gp.tensor_tensor(wo[0][:, k, 1, :], out_raw[0][:, n, :], wo[0][:, k, 0, :].bitcast(F32), ALU.subtract).then_inc(out_lo, 1)

            def ln_affine(kind):
                i1 = LN[kind]["i1"]
                gb = (gb_mid if kind.startswith("mid") else gb_end)[0 if kind.endswith("0") else 1]
                gp.wait_ge(gb_ld, 32 * (i1 + 1))

                def step(s):
                    if s.live(0):
                        gp.wait_ge(norm1, s.tile(0) + (NT * i1 + 1))
                        y = ln_y[:, s.slot(0), :]
                        gp.tensor_tensor(y, y, gb[:, 0, :], ALU.mult).then_inc(g_mul, 1)
                        gp.wait_ge(g_mul, s.tile(0) + (NT * i1 + 1))
                        gp.tensor_tensor(y, y, gb[:, 1, :], ALU.add).then_inc(x1_rdy, 1)
                ln_steps(gp, step)

            def clear_acc(l):
                gp.wait_ge(out_done, NT * (l + 1))
                gp.memset(acc[l][:], 0.0).then_inc(acc_zero, 1)

            def clear_pads(line, after):
                gp.wait_ge(act_rdy, after)
                gp.memset(line[:, 0:1], 0.0)
                gp.memset(line[:, CTX + 1:CTX + 2], 0.0)
                gp.memset(line[:, PADW - 2:PADW], 0.0).then_inc(pads, 1)

            out_split()
            ln_affine("mid0")
            clear_acc(0)
            clear_pads(f_a, 2 * NT)
            ln_affine("end0")
            gp.wait_ge(brow_mm, 8)
            clear_pads(c_p, 3 * NT)
            ln_affine("mid1")
            clear_acc(1)
            clear_pads(f_a, 4 * NT)
            ln_affine("end1")

        @block.scalar
        def _(act):
            def copy(o, i):
                return act.activation(o, i, ACT.Copy)

            act.wait_ge(setup_t, 4)
            copy(par[:], ps[:, 0, 0:220]).then_inc(setup_c, 1)
            act.activation(conds[:].rearrange("p k c -> p c k"), ps[:, 0, 204:220].rearrange("p (c k) -> p c k", c=2), ACT.Silu).then_inc(setup_c, 1)

            def d_hi_at(slot, count, dst, width=D):
                act.wait_ge(d_loaded[slot], count * 16)
                copy(dst, raw_d[:, slot, 0:width]).then_inc(d_hi, 1)

            def ada_evac(m, i=None):
                l, half = ada_half(m)
                used = ADA_SLOTS + 4 * m + 4
                col = half * 512 if i is None else i * 1536 + half * 512
                act.wait_ge(ada_used, used if i is None else i * 12 + used)
                act.wait_ge(ada_st[m % 3], 16 * (m // 3 + 1) if i is None else i * 16 + 16 * (m // 3 + 1))
                copy(ada_row[0:2, m % 3, :], ps[0:2, m % 3, :]).then_inc(ada_bank, 1)
                act.wait_ge(ada_bank, m + 4 if i is None else i * 3 + (m + 4))
                act.dma_start(ada[l, :, bass.ds(col, 512)], ada_row[0:2, m % 3, :]).then_inc(ada_st[m % 3], 16)

            def u_hi_at(n, half, slot):
                act.wait_ge(u_loaded[slot], half * 16 + 16)
                act.wait_ge(up_done, n * 3 + 3)
                copy(uw[:, slot, 0, :, :], raw_u[:, slot, :, :]).then_inc(u_hi, 1)

            for m in range(4):
                ada_evac(m)
            for n in range(2):
                u_hi_at(n, 0, n)

            def ln_act(kind, dest):
                i1, i4 = LN[kind]["i1"], LN[kind]["i4"]
                l = 0 if kind in ("in", "mid0") else 1
                c0 = 0 if kind in ("in", "end0") else 2

                def gate(k):
                    act.wait_ge(gate_mm, 2 * i1 + k)
                    if k == 2:
                        act.wait_ge(out_evac, NT * i1 + 1)
                    copy(ln_g[:].rearrange("p (a n) -> p a n", a=2), ps[:, 6:8, :]).then_inc(gate_rdy, 1)

                def step(s):
                    if i4 is not None and s.live(2):
                        tile = s.tile(2)
                        cc = 1 if s.first(2) else 0
                        if s.first(2):
                            act.wait_ge(cols_done, {"in": 2, "mid0": 4, "end0": 6, "mid1": 8}[kind])
                        act.wait_ge(zt_done, tile + (NT * i4 + 1))
                        if not s.first(2):
                            act.wait_ge(act_rdy, tile + NT * i4)
                        for k in range(KD):
                            o = act.activation(ln_u[:, k * P:(k + 1) * P], ps[:, 6 + k // 4, (k % 4) * P:(k % 4 + 1) * P],
                                               ACT.Identity, bias=cols[:, l, c0, k, cc:cc + 1], scale=cols[:, l, c0 + 1, k, cc:cc + 1])
                        o.then_inc(mod_done, 1)
                    if i1 is not None and s.live(0):
                        if s.first(0):
                            gate(2)
                        st = stats[:, s.slot(0), :]
                        act.wait_ge(stat1, s.tile(0) + (NT * i1 + 1))
                        act.activation(st[:, 14:15], st[:, 13:14], ACT.Sqrt, bias=eps, scale=1.0).then_inc(sd1, 1)
                        act.wait_ge(rs1, s.tile(0) + (NT * i1 + 1))
                        y = ln_y[:, s.slot(0), :]
                        act.activation(y, y, ACT.Identity, bias=st[:, 16:17], scale=st[:, 15:16]).then_inc(norm1, 1)
                    if i4 is not None and s.live(1):
                        st = stats[:, s.slot(1), :]
                        act.wait_ge(stat2, s.tile(1) + (NT * i4 + 1))
                        act.activation(st[:, 34:35], st[:, 33:34], ACT.Sqrt, bias=eps, scale=1.0).then_inc(sd2, 1)

                    def rounding():
                        if i4 is not None and s.live(2):
                            tile = s.tile(2)
                            act.wait_ge(mod_done, tile + (NT * i4 + 1))
                            copy(dest[:, :, 0, bass.ds(tile * P, P)], ln_u[:].rearrange("p (k t) -> p k t", k=KD)).then_inc(act_hi, 1)

                    if i1 is not None:
                        rounding()
                    if i4 is not None and s.live(1):
                        tile = s.tile(1)
                        act.wait_ge(rs2, tile + (NT * i4 + 1))
                        if not s.first(1):
                            act.wait_ge(zt_done, tile + NT * i4)
                        st = stats[:, s.slot(1), :]
                        act.activation(ln_z[:], ln_y[:, s.slot(1), :], ACT.Identity, bias=st[:, 36:37], scale=st[:, 35:36]).then_inc(z_rdy, 1)
                    if i1 is None:
                        rounding()
                    for m in ada_steps(kind).get(s.base, []):
                        ada_evac(m, s.i)

                if i1 is not None:
                    gate(1)
                ln_steps(act, step)

            ln_act("in", act_a)

            act.wait_ge(pp_zero, 1)
            act.wait_ge(ada_used, ADA_SLOTS + 64)
            for n in range(NPG):
                if n in (1, 2):
                    u_hi_at(n + 1, (n + 1) // 2, (n + 1) % 2)
                for k in (2 * n, 2 * n + 1):
                    d_hi_at(k % 2, k // 2 + 1, wq[:, k, 0, :], AW)
                for c in range(NCH):
                    act.wait_ge(up_done, 6 + 3 * n + c + 1)
                    for u0, ln, p0 in PPIECES[c]:
                        o = copy(pp[:, n, p0:p0 + ln], ps[:, 3 * (n % 2) + c, u0 - c * CH:u0 - c * CH + ln])
                    o.then_inc(bank_free[n % 2], 1)
            for k in range(KD // 2):
                n = D_QKV + KD + k
                act.wait_ge(d_loaded[n % 2], 16 * (n // 2 + 1))
                copy(wkv[:, 2 * k:2 * k + 2, 0, :], raw_d[:, n % 2, 0:512].rearrange("p (a n) -> p a n", a=2)).then_inc(d_hi, 1)

            def heads(ap):
                return ap.rearrange("p (h d) -> p h d", d=HD)

            def k_round(src):
                copy(k4[:, :, 0, :].bitcast(F32R), src).then_inc(k_hi, 1)

            def kt_evac(idx, kb, bank):
                act.wait_ge(kt_tr, idx + 1)
                copy(kt[:, :, bass.ds(kb * P, P)], ps[:, 4 + bank, 0:256].rearrange("p (v t) -> p v t", v=2)).then_inc(kt_ev, 1)

            def qkv_tile(tile, par2, ctx_tile):
                qb, vb = 2 * par2, 2 * par2 + 1
                act.wait_ge(qkv_done, tile + 1)
                if not ctx_tile:
                    act.wait_ge(k_rdy, tile)
                act.activation(sq[:, 0:NH, :], heads(ps[:, qb, :]), ACT.Square)
                act.activation(sq[:, NH:, :], heads(ps[:, vb, 0:P]), ACT.Square).then_inc(sq_done, 1)
                if ctx_tile:
                    copy(kv_out[:, 1, :], ps[:, vb, P:2 * P]).then_inc(v_out, 1)
                kb = LKB if ctx_tile else tile - 1
                copy(vhl[:, bass.ds(kb, 1), :, 0, :].rearrange("p a v d -> p (a v) d"), heads(ps[:, vb, P:2 * P])).then_inc(v_hi, 1)
                act.wait_ge(ss_done, tile + 1)
                act.activation(small[:, 32:42], small[:, 20:30], ACT.Sqrt, bias=eps, scale=1.0 / HD).then_inc(qsd, 1)
                act.wait_ge(k_rdy, tile + 1)
                if ctx_tile:
                    k_round(heads(kv_out[:, 0, :]))
                    kt_evac(0, LKB, 0)
                    act.wait_ge(past_ld, 32)
                    k_round(heads(kv_past[:, 0, :]))
                    copy(vhl[:, LKB - 1, :, 0, :], heads(kv_past[:, 1, :])).then_inc(v_hi, 1)
                    kt_evac(1, LKB - 1, 1)
                else:
                    k_round(xk[:])
                    kt_evac(tile + 1, tile - 1, 1 - par2)

            qkv_tile(0, 0, True)
            with act.Fori(0, NQ // 2) as i:
                for j in range(2):
                    qkv_tile(i * 2 + (j + 1), 1 - j, False)

            act.wait_ge(k_lo, NT + 1)
            d_hi_at(D_WPOOL % 2, D_WPOOL // 2 + 1, wp[:, 0, :, :].rearrange("p g d -> p (g d)"), NPG * P)

            def qs_round(tile, j):
                if not (tile.ctx and j == 0):
                    act.wait_ge(qt_tr, tile.unit0 + j)
                kv = j % 2
                if tile.ctx:
                    src = q_ctx[:, kv * G:(kv + 1) * G, :]
                else:
                    src = q_lat[:, bass.ds(tile.q + j // 2, 1), kv * 256:(kv + 1) * 256].rearrange("p a (h d) -> p (a h) d", h=G)
                copy(qs[:, :, 0, 0, :].bitcast(F32R), src)
                copy(qs[:, :, 0, 1, :].bitcast(F32R), src).then_inc(qs_hi, 1)

            def qt_evac(tile, j):
                act.wait_ge(qt_tr, tile.unit0 + (j + 1))
                for r in range(2):
                    bank = tile.bank(("q", j, r))
                    copy(qt[:, j % 2, 2 * r:2 * r + 2, :, :].rearrange("p h a t -> p (h a t)"), ps[:, 6 + bank, :]).then_inc(t_free[bank], 1)

            def first(tile):
                if tile.ctx:
                    act.wait_ge(qkv_free, NT)
                qs_round(tile, 0)
                qt_evac(tile, 0)

            def step(tile, s):
                def round_turned(r):
                    h, nb = s - 2, min(3, tile.nk)
                    act.wait_ge(tr_done, tile.round0 + (tile.rounds * h + r + 1))
                    copy(pt[:, 0, 3 * r:3 * r + nb, h % 4, :], ps[:, 6 + tile.bank(("t", h, r)), 0:nb * P].rearrange("p (b t) -> p b t", b=nb)).then_inc(th_hi, 1)

                def exponentials(h):
                    act.wait_ge(mx_done, tile.head0 + (h + 1))
                    if tile.ctx:
                        if h >= 4:
                            act.wait_ge(tr_done, h - 3)
                    elif tile.first and h < 4:
                        act.wait_ge(tr_done, NH + h - 3)
                    else:
                        act.wait_ge(tr_done, tile.round0 + 3 * (h - 3))
                    nb, nw = (3, CH) if tile.nk > 1 else (1, P)
                    b0 = 3 * (h % 2)
                    act.activation(prob[:, h % 4, 0:nb * nw].rearrange("p (b n) -> p b n", b=nb), ps[:, b0:b0 + nb, 0:nw],
                                   ACT.Exp, bias=small[:, h % 4:h % 4 + 1], scale=1.0, accum_out=small[:, 8 + h % 4:9 + h % 4]).then_inc(exp_done, 1)

                j = tile.output(s)
                if j is not None and has_exp(tile, s):
                    exponentials(s)
                if j is not None:
                    un = tile.unit0 + j
                    act.wait_ge(pv_done, un + 1)
                    copy(o_t[0:HD, :, :], ps[HD:P, 6 + tile.bank(("o", j, 0)), :].rearrange("p (h t) -> p h t", h=G)).then_inc(o_cp, 1)
                rounds = range(tile.rounds) if has_trans(s) else ()
                for r in rounds[:2]:
                    round_turned(r)
                if j is None and has_exp(tile, s):
                    exponentials(s)
                for r in rounds[2:]:
                    round_turned(r)
                if tile.turns(s):
                    qt_evac(tile, (s - 1) // 4 + 1)
                if j is not None:
                    act.wait_ge(o_sum, un + 1)
                    tile.wait_evac(act, ("o", j, 0))
                    tk = 0 if tile.ctx else tile.q if j < 0 else tile.q + 1
                    copy(act_b[:, 2 * (j % 2):2 * (j % 2) + 2, 0, bass.ds(tk * P, P)], o_f[:]).then_inc(m_hi, 1)
                if tile.splits(s):
                    qs_round(tile, s // 4 + 1)

            att_steps(act, step, first)

            act.wait_ge(pool_done, 1)
            act.wait_ge(m_att, 2 + 2 * NQ)
            for g in range(NPG):
                for start, u0, n in ((8, 0, CTX), (CTX + 16, CTX, LAT)):
                    o = copy(ph[:, g, 0, u0:u0 + n], pp[:, g, start:start + n])
                o.then_inc(ph_hi, 1)

            def wo_hi(l, k, d0):
                if k in OUT_EXTRA and l == 0:
                    return
                if k in OUT_EXTRA:
                    act.wait_ge(out_ld, 64 * 2)
                    copy(wo[l][:, k, 0, :], out_raw[l][:, k - OUT_EXTRA[0], :]).then_inc(out_hi, 1)
                    return
                n = d0 + (k if k < 2 else k - 4)
                d_hi_at(n % 2, n // 2 + 1, wo[l][:, k, 0, :])

            for g in range(NPG):
                wo_hi(0, g, D_OUT0)
                act.wait_ge(mix_done, g + 1)
                if g == 0:
                    act.wait_ge(ph_lo, NPG)
                else:
                    act.wait_ge(mix_lo, g)
                act.activation(mf[:].rearrange("p (c n) -> p c n", c=NCH), ps[:, 3 * (g % 2):3 * (g % 2) + 3, 0:CH],
                               ACT.Identity, bias=0.0, scale=par[:, 200 + g:201 + g]).then_inc(mix_ev, 1)
                act.wait_ge(mix_ev, g + 1)
                copy(act_b[:, 4 + g, 0, :], mf[:]).then_inc(mix_hi, 1)
            for k in range(4, KD):
                wo_hi(0, k, D_OUT0)

            class Ffn:
                def __init__(self, l, u0, d0):
                    self.l, self.u0, self.d0 = l, u0, d0

                def hi_u(self, g, j):
                    u_hi_at(g * 4 + (self.u0 + j), g * 2 + (self.u0 // 2 + j // 2), j % 2)

                def body(self, g, last):
                    l, u0, d0 = self.l, self.u0, self.d0
                    hh_, ft, fs, fh = hh[l], f_t[l], f_s[l], f_h[l]
                    for b in range(2):
                        self.hi_u(g, 2 * b + 1)
                        q = g * 2 + (NF * l + b)
                        act.wait_ge(conv_done, q + 1)
                        for c in range(NCH):
                            act.wait_ge(up_done, g * 12 + (6 + 3 * (u0 + 2 * b) + c + 1))
                            for s0, ln, p0 in PIECES[c]:
                                o = copy(f_a[:, p0:p0 + ln], ps[:, c, s0 - c * CH:s0 - c * CH + ln])
                            o.then_inc(bank_free[0], 1)
                        if b == 0:
                            self.hi_u(g, 2)
                            if l or not isinstance(g, int) or g:
                                act.wait_ge(down_done, g * 18 + 18 * NG * l)
                            for j in range(2):
                                d_hi_at((d0 + j) % 2, g + ((d0 + j) // 2 + 1), dw[:, j, 0, :])
                        elif not last:
                            self.hi_u(g + 1, 0)
                        act.wait_ge(conv_done, q + 2)
                        act.wait_ge(h_mul, q * 3 + 3)
                        act.activation(fs[:, 1:PADW - 2], ft[:, 1:PADW - 2], ACT.Silu).then_inc(silu_done, 1)
                        for c in range(NCH):
                            act.wait_ge(h_mul, q * 3 + (c + 4))
                            copy(hh_[:, b, 0, c * CH:(c + 1) * CH], fh[:, c * CH:(c + 1) * CH]).then_inc(h_hi, 1)

                def run(self):
                    for j in range(3):
                        act.wait_ge(x_st[j], 48 * (2 * self.l + 1))
                    act.wait_ge(pads, 1 + 2 * self.l)
                    self.body(0, False)
                    with act.Fori(1, NG - 1) as g:
                        self.body(g, False)
                    self.body(NG - 1, True)

            f = Ffn(0, U_FFN0, D_DOWN0)
            act.wait_ge(out_lo, 4)
            f.hi_u(0, 0)
            ln_act("mid0", act_b)
            f.run()
            u_hi_at(U_FOUR, U_FOUR // 2, 0)
            ln_act("end0", act_b)

            for j in range(3):
                act.wait_ge(x_st[j], 48 * 2)
            act.wait_ge(act_rdy, 3 * NT)
            d_hi_at(D_CHAN % 2, D_CHAN // 2 + 1, chan[:, 0, :], 2 * P)
            u_hi_at(U_FOUR + 1, U_FOUR // 2, 1)
            for b in range(FB):
                if b:
                    u_hi_at(U_CONV, U_CONV // 2, 0)
                for c in range(NCH):
                    act.wait_ge(up_done, 6 + 3 * (U_FOUR + b) + c + 1)
                    copy(f_in[:, b, 0, c * CH:(c + 1) * CH], ps[:, 3 * b + c, 0:CH]).then_inc(fi_hi, 1)
            d_hi_at(D_CTAB % 2, D_CTAB // 2 + 1, dw[:, 0, 0, 0:2 * P], 2 * P)
            for tile in range(NT):
                act.wait_ge(fc_done, tile + 1)
                copy(f_ch[:, tile, 0, :], ps[:, 6 + tile % 2, :]).then_inc(fc_hi, 1)
            for k in range(16):
                act.wait_ge(d_used, 2 + k)
                d_hi_at((D_TAB + k) % 2, (D_TAB + k) // 2 + 1, dw[:, (k + 1) % 2, 0, :])
            for b in range(FB):
                for h in range(3):
                    if b == 0:
                        act.wait_ge(d_used, 3 if h == 0 else 3 + 16)
                    if h == 0:
                        o, i = act_a[:, CB + b, 0, 0:CTX], ps[:, 4 + b, 0:P]
                    else:
                        o, i = act_a[:, CB + b, 0, CTX + 512 * (h - 1):CTX + 512 * h], ps[:, 2 * b + h - 1, :]
                    copy(o, i).then_inc(pos_hi, 1)

            with act.Fori(0, CB // 2) as i:
                for j in range(2):
                    b = i * 2 + j
                    u_hi_at(*conv_unit(i, 3 * j + 1))
                    act.wait_ge(cp_rdy, b * 3 + 3)
                    n = conv_unit(i, 3 * j)[0]
                    for c in range(NCH):
                        act.wait_ge(up_done, n * 3 + (6 + c + 1))
                        copy(c_h[:, c * CH:(c + 1) * CH], ps[:, 3 * j + c, 0:CH]).then_inc(ch_rdy, 1)
                    u_hi_at(*conv_unit(i, 3 * j + 2))
                    u_hi_at(*conv_unit(i, 3 * j + 3))
                    for c in range(NCH):
                        act.wait_ge(cm_rdy, b * 3 + (c + 4))
                        copy(act_a[:, bass.ds(b, 1), 0, c * CH:(c + 1) * CH].rearrange("p a n -> p (a n)"), c_m[:, c * CH:(c + 1) * CH]).then_inc(cm_hi, 1)
            for k in range(KD):
                wo_hi(1, k, D_OUT1)
            ln_act("mid1", act_a)
            Ffn(1, U_FFN1, D_DOWN1).run()
            ln_act("end1", None)

        @block.vector
        def _(v):
            class Chain:
                def __init__(self):
                    self.n, self.i, self.per, self.start = 0, None, 0, 0

                def __call__(self, ins):
                    self.n += 1
                    ins.then_inc(v_step, 1)
                    v.wait_ge(v_step, self.n if self.i is None else self.i * self.per + self.n)

                def enter(self, i, per):
                    self.i, self.per, self.start = i, per, self.n

                def leave(self, passes):
                    assert self.n - self.start == self.per, (self.n - self.start, self.per)
                    self.n, self.i = self.start + passes * self.per, None

            chain = Chain()

            def lo(dst, src, hi):
                return v.tensor_tensor(dst, src, hi.bitcast(F32), ALU.subtract)

            def heads(ap):
                return ap.rearrange("p (h d) -> p h d", d=HD)

            def d_lo_at(n, slot, dst, hi, width=D, g=None):
                v.wait_ge(d_hi, n + 1 if g is None else g * 2 + (n + 1))
                lo(dst, raw_d[:, slot, 0:width], hi).then_inc(d_split, 1)

            def u_lo_at(n, half, slot):
                v.wait_ge(u_hi, n + 1)
                lo(uw[:, slot, 1, :, :], raw_u[:, slot, :, :], uw[:, slot, 0, :, :]).then_inc(u_split, 1)

            def cols_of(ns):
                for n in ns:
                    l, j = n // 4, n % 4
                    v.wait_ge(brow_mm, n + 1)
                    v.tensor_scalar(cols[:, l, j, :, :].rearrange("p k c -> p (k c)"), ps[:, 6 + n % 2, 0:16],
                                    1.0 if j % 2 else 0.0, None, ALU.add).then_inc(cols_done, 1)

            u_lo_at(0, 0, 0)
            u_lo_at(1, 0, 1)
            cols_of(range(2))

            def norm_stats(x, st, o):
                for h in range(2):
                    r = v.bn_stats(st[:, o + 6 * h:o + 6 * h + 6], x[:, 512 * h:512 * (h + 1)])
                chain(r)
                v.tensor_copy(st[:, o + 17:o + 19], st[:, o:o + 2])
                return v.bn_aggr(st[:, o + 12:o + 14], st[:, o:o + 12])

            def norm_scale(st, o):
                chain(v.reciprocal(st[:, o + 15:o + 16], st[:, o + 14:o + 15]))
                return v.tensor_scalar(st[:, o + 16:o + 17], st[:, o + 12:o + 13], st[:, o + 15:o + 16], -1.0, ALU.mult, ALU.mult)

            def ln_vec(kind, dest, src):
                ph_, i1, i4, im = (LN[kind][x] for x in ("ph", "i1", "i4", "im"))

                def step(s):
                    if i1 is not None and s.live(0):
                        tile, slot = s.tile(0), s.slot(0)
                        y, st = ln_y[:, slot, :], stats[:, slot, :]
                        if im is not None:
                            v.wait_ge(out_done, tile + (NT * im + 1))
                        if s.first(0):
                            v.wait_ge(gate_rdy, 2 * i1 + 1)
                        if s.i is None and s.base == 1:
                            v.wait_ge(gate_rdy, 2 * i1 + 2)
                        o, x = src(tile, slot)
                        v.tensor_tensor(ln_t[:].rearrange("p (a n) -> p a n", a=o), x, ln_g[:].rearrange("p (a n) -> p a n", a=o), ALU.mult).then_inc(out_evac, 1)
                        v.wait_ge(out_evac, tile + (NT * i1 + 1))
                        v.wait_ge(x_ld[slot], s.third(0) * 16 + (48 * ph_ + 16))
                        chain(v.scalar_tensor_tensor(y, y, ALPHA, ln_t[:], ALU.mult, ALU.add))
                        norm_stats(y, st, 0).then_inc(stat1, 1)
                        v.wait_ge(sd1, tile + (NT * i1 + 1))
                        norm_scale(stats[:, slot, :], 0).then_inc(rs1, 1)
                    if i4 is not None and s.live(1):
                        tile, slot = s.tile(1), s.slot(1)
                        if i1 is not None:
                            v.wait_ge(x1_rdy, tile + (NT * i1 + 1))
                        else:
                            v.wait_ge(x_ld[slot], s.third(1) * 16 + (48 * ph_ + 16))
                        norm_stats(ln_y[:, slot, :], stats[:, slot, :], 20).then_inc(stat2, 1)
                        v.wait_ge(sd2, tile + (NT * i4 + 1))
                        norm_scale(stats[:, slot, :], 20).then_inc(rs2, 1)
                    if i4 is not None and s.live(2):
                        tile = s.tile(2)
                        v.wait_ge(act_hi, tile + (NT * i4 + 1))
                        lo(dest[:, :, 1, bass.ds(tile * P, P)], ln_u[:].rearrange("p (k t) -> p k t", k=KD), dest[:, :, 0, bass.ds(tile * P, P)]).then_inc(act_rdy, 1)

                def loop(i):
                    if i is None:
                        chain.leave(2)
                    else:
                        chain.enter(i, 3 * ((3 if i1 is not None else 0) + (2 if i4 is not None else 0)))
                ln_steps(v, step, loop)

            def from_psum(tile, slot):
                return 2, ps[:, 2 * slot:2 * slot + 2, :]

            def from_acc(l):
                return lambda tile, slot: (1, acc[l][:, bass.ds(tile, 1), :])

            ln_vec("in", act_a, None)

            for n in range(NPG):
                if n in (1, 2):
                    u_lo_at(n + 1, (n + 1) // 2, (n + 1) % 2)
                for k in (2 * n, 2 * n + 1):
                    d_lo_at(D_QKV + k, k % 2, wq[:, k, 1, :], wq[:, k, 0, :], AW)
                if n in (1, 3):
                    cols_of(range(n + 1, n + 3))
            for k in range(KD // 2):
                n = D_QKV + KD + k
                v.wait_ge(d_hi, n + 1)
                lo(wkv[:, 2 * k:2 * k + 2, 1, :], raw_d[:, n % 2, 0:512].rearrange("p (a n) -> p a n", a=2), wkv[:, 2 * k:2 * k + 2, 0, :]).then_inc(d_split, 1)
            v.wait_ge(g_ld, 32)
            chain(v.tensor_scalar(g_row[:, 0, :], g_row[:, 0, :], HD ** -0.5, None, ALU.mult))

            def k_lo_of(idx, src):
                v.wait_ge(k_hi, idx + 1)
                lo(k4[:, :, 1, :].bitcast(F32R), src, k4[:, :, 0, :]).then_inc(k_lo, 1)

            def gains(kind, n):
                return g_row[:, kind, :].unsqueeze(1).broadcast_to([P, n, HD])

            def qkv_tile(tile, par2, ctx_tile, half=None):
                qb, vb = 2 * par2, 2 * par2 + 1
                v.wait_ge(sq_done, tile + 1)
                v.tensor_reduce(small[:, 20:30], sq[:], AX_X, ALU.add).then_inc(ss_done, 1)
                v.wait_ge(qsd, tile + 1)
                chain(v.reciprocal(small[:, 44:54], small[:, 32:42]))
                v.tensor_tensor(xn[:, 0:NH, :], heads(ps[:, qb, :]), small[:, 44:52].unsqueeze(2).broadcast_to([P, NH, HD]), ALU.mult)
                chain(v.tensor_tensor(xn[:, NH:, :], heads(ps[:, vb, 0:P]), small[:, 52:54].unsqueeze(2).broadcast_to([P, NKV, HD]), ALU.mult))
                kb = LKB if ctx_tile else tile - 1
                v.wait_ge(v_hi, 1 if ctx_tile else tile + 2)
                lo(vhl[:, bass.ds(kb, 1), :, 1, :].rearrange("p a v d -> p (a v) d"), heads(ps[:, vb, P:2 * P]),
                   vhl[:, bass.ds(kb, 1), :, 0, :].rearrange("p a v d -> p (a v) d")).then_inc(qkv_free, 1)
                if ctx_tile:
                    v.tensor_tensor(q_ctx[:], xn[:, 0:NH, :], gains(0, NH), ALU.mult)
                    v.tensor_tensor(heads(kv_out[:, 0, :]), xn[:, NH:, :], gains(1, NKV), ALU.mult).then_inc(k_rdy, 1)
                    k_lo_of(0, heads(kv_out[:, 0, :]))
                    k_lo_of(1, heads(kv_past[:, 0, :]))
                    v.wait_ge(v_hi, 2)
                    chain(lo(vhl[:, LKB - 1, :, 1, :], heads(kv_past[:, 1, :]), vhl[:, LKB - 1, :, 0, :]))
                    return
                v.tensor_tensor(xn[:, 0:NH, :], xn[:, 0:NH, :], gains(0, NH), ALU.mult)
                chain(v.tensor_tensor(xn[:, NH:, :], xn[:, NH:, :], gains(1, NKV), ALU.mult))
                slot = 1 - par2
                v.wait_ge(rope_ld[slot], half * 16 + 16)
                v.tensor_tensor(rope_a[:], xn[:], rope_t[:, slot, 0, :].unsqueeze(1).broadcast_to([P, NH + NKV, HD]), ALU.mult)
                pairs = "p h (e two) -> p h e two"
                for two in range(2):
                    o = v.tensor_tensor(rope_b[:].rearrange(pairs, two=2)[:, :, :, two], xn[:].rearrange(pairs, two=2)[:, :, :, 1 - two],
                                        rope_t[:, slot, 1, :].rearrange("p (e two) -> p e two", two=2)[:, :, two].unsqueeze(1)
                                        .broadcast_to([P, NH + NKV, HD // 2]), ALU.mult)
                chain(o)
                v.tensor_tensor(heads(q_lat[:, bass.ds(tile - 1, 1), :].rearrange("p a n -> p (a n)")), rope_a[:, 0:NH, :], rope_b[:, 0:NH, :], ALU.add)
                v.tensor_tensor(xk[:], rope_a[:, NH:, :], rope_b[:, NH:, :], ALU.add).then_inc(k_rdy, 1)
                k_lo_of(tile + 1, xk[:])

            v.wait_ge(past_ld, 32)
            qkv_tile(0, 0, True)
            with v.Fori(0, NQ // 2) as i:
                chain.enter(i, 8)
                for j in range(2):
                    qkv_tile(i * 2 + (j + 1), 1 - j, False, i)
            chain.leave(NQ // 2)

            flat = "p g d -> p (g d)"
            d_lo_at(D_WPOOL, D_WPOOL % 2, wp[:, 1, :, :].rearrange(flat), wp[:, 0, :, :].rearrange(flat), NPG * P)

            def qs_split(tile, j):
                v.wait_ge(qs_hi, tile.unit0 + (j + 1))
                kv = j % 2
                if tile.ctx:
                    src = q_ctx[:, kv * G:(kv + 1) * G, :]
                else:
                    src = q_lat[:, bass.ds(tile.q + j // 2, 1), kv * 256:(kv + 1) * 256].rearrange("p a (h d) -> p (a h) d", h=G)
                lo(qs[:, :, 1, 0, :].bitcast(F32R), src, qs[:, :, 0, 0, :])
                lo(qs[:, :, 1, 1, :].bitcast(F32R), src, qs[:, :, 0, 1, :]).then_inc(qs_lo, 1)

            def step(tile, s):
                def split_turned(r):
                    h, nb = s - 2, min(3, tile.nk)
                    bank = tile.bank(("t", h, r))
                    v.wait_ge(th_hi, tile.round0 + (tile.rounds * h + r + 1))
                    lo(pt[:, 1, 3 * r:3 * r + nb, h % 4, :], ps[:, 6 + bank, 0:nb * P].rearrange("p (b t) -> p b t", b=nb),
                       pt[:, 0, 3 * r:3 * r + nb, h % 4, :]).then_inc(t_free[bank], 1)

                def inverse_sum():
                    v.wait_ge(exp_done, tile.head0 + (s + 1))
                    v.reciprocal(small[:, 16 + s % 4:17 + s % 4], small[:, 8 + s % 4:9 + s % 4]).then_inc(rinv_done, 1)

                def maximum(h):
                    nb, nw = (3, CH) if tile.nk > 1 else (1, P)
                    b0 = 3 * (h % 2)
                    v.wait_ge(s_done, tile.head0 + (h + 1))
                    v.tensor_reduce(small[:, h % 4:h % 4 + 1], ps[:, b0:b0 + nb, 0:nw], mybir.AxisListType.XY, ALU.max, negate=True).then_inc(mx_done, 1)

                j = tile.output(s)
                if j is not None:
                    if has_exp(tile, s):
                        inverse_sum()
                    if has_score(tile, s):
                        maximum(s + 1)
                    un, bank = tile.unit0 + j, tile.bank(("o", j, 0))
                    v.wait_ge(o_cp, un + 1)
                    for odd, done in ((0, o_sum), (1, t_free[bank])):
                        v.tensor_tensor(o_f[HD * odd:HD * odd + HD, :, :],
                                        ps[0:HD, 6 + bank, :].rearrange("p (a h t) -> p a h t", h=2, t=P)[:, :, odd, :],
                                        o_t[0:HD, :, :].rearrange("p (a h) t -> p a h t", h=2)[:, :, odd, :], ALU.add).then_inc(done, 1)
                rounds = range(tile.rounds) if has_trans(s) else ()
                for r in rounds[:1]:
                    split_turned(r)
                if j is None and has_score(tile, s):
                    maximum(s + 1)
                for r in rounds[1:2]:
                    split_turned(r)
                if j is None and has_exp(tile, s):
                    inverse_sum()
                for r in rounds[2:]:
                    split_turned(r)
                if j is not None:
                    v.wait_ge(m_hi, un + 1)
                    tk = 0 if tile.ctx else tile.q if j < 0 else tile.q + 1
                    blocks = slice(2 * (j % 2), 2 * (j % 2) + 2)
                    lo(act_b[:, blocks, 1, bass.ds(tk * P, P)], o_f[:], act_b[:, blocks, 0, bass.ds(tk * P, P)]).then_inc(m_att, 1)
                if tile.splits(s):
                    qs_split(tile, s // 4 + 1)

            att_steps(v, step, lambda tile: qs_split(tile, 0))

            for g in range(NPG):
                v.wait_ge(ph_hi, g + 1)
                for start, u0, n in ((8, 0, CTX), (CTX + 16, CTX, LAT)):
                    o = lo(ph[:, g, 1, u0:u0 + n], pp[:, g, start:start + n], ph[:, g, 0, u0:u0 + n])
                o.then_inc(ph_lo, 1)

            def wo_lo(l, k, d0):
                if k in OUT_EXTRA and l == 1:
                    v.wait_ge(out_hi, 4 + k - OUT_EXTRA[0] + 1)
                    lo(wo[l][:, k, 1, :], out_raw[l][:, k - OUT_EXTRA[0], :], wo[l][:, k, 0, :]).then_inc(out_lo, 1)
                    return
                if k in OUT_EXTRA:
                    v.wait_ge(out_ld, 64)
                    if k < 4:
                        v.wait_ge(m_att, 2 + 2 * NQ)
                    else:
                        v.wait_ge(mix_done, NPG)
                    v.tensor_copy(wo[l][:, k, 0, :], out_raw[l][:, k - OUT_EXTRA[0], :]).then_inc(out_hi, 1)
                    return
                n = d0 + (k if k < 2 else k - 4)
                d_lo_at(n, n % 2, wo[l][:, k, 1, :], wo[l][:, k, 0, :])

            for g in range(NPG):
                wo_lo(0, g, D_OUT0)
                v.wait_ge(mix_hi, g + 1)
                lo(act_b[:, 4 + g, 1, :], mf[:], act_b[:, 4 + g, 0, :]).then_inc(mix_lo, 1)
            for k in range(4, KD):
                wo_lo(0, k, D_OUT0)

            def conv3(dst, line, w, done):
                n = PADW - 3
                chain(v.tensor_scalar(dst[:, 1:1 + n], line[:, 0:n], w(0), w(3), ALU.mult, ALU.add))
                chain(v.scalar_tensor_tensor(dst[:, 1:1 + n], line[:, 1:1 + n], w(1), dst[:, 1:1 + n], ALU.mult, ALU.add))
                o = v.scalar_tensor_tensor(dst[:, 1:1 + n], line[:, 2:2 + n], w(2), dst[:, 1:1 + n], ALU.mult, ALU.add)
                if done is None:
                    chain(o)
                else:
                    o.then_inc(done, 1)

            class Ffn:
                def __init__(self, l, u0, d0):
                    self.l, self.u0, self.d0 = l, u0, d0

                def lo_u(self, g, j):
                    u_lo_at(g * 4 + (self.u0 + j), None, j % 2)

                def body(self, g, last):
                    l, u0, d0 = self.l, self.u0, self.d0
                    taps = par[:, 88 * l:88 * l + 88].rearrange("p (j f) -> p j f", j=4)
                    chain(v.tensor_copy(fgrp[:], taps[:, :, bass.ds(g * 2, 2)]))
                    for b in range(2):
                        q = g * 2 + (NF * l + b)
                        self.lo_u(g, 2 * b + 1)
                        r = 2 + (NF + 1) * l + b
                        v.wait_ge(bank_free[0], g * 6 + (3 * r + 6))
                        v.wait_ge(silu_done, q + 1)
                        conv3(f_t[l], f_a, lambda j: fgrp[:, j, b:b + 1], conv_done)
                        if b == 0:
                            self.lo_u(g, 2)
                            for j in range(2):
                                d_lo_at(d0 + j, (d0 + j) % 2, dw[:, j, 1, :], dw[:, j, 0, :], g=g)
                        elif not last:
                            self.lo_u(g + 1, 0)
                        v.wait_ge(silu_done, q + 2)

                        def mult(c):
                            v.wait_ge(up_done, g * 12 + (6 + 3 * (u0 + 2 * b + 1) + c + 1))
                            for s0, ln, p0 in PIECES[c]:
                                o = v.tensor_tensor(f_h[l][:, s0:s0 + ln], f_s[l][:, p0:p0 + ln], ps[:, 3 + c, s0 - c * CH:s0 - c * CH + ln], ALU.mult)
                            o.then_inc(h_mul, 1)

                        def h_split(c):
                            v.wait_ge(h_hi, q * 3 + (c + 1))
                            sl = slice(c * CH, (c + 1) * CH)
                            lo(hh[l][:, b, 1, sl], f_h[l][:, sl], hh[l][:, b, 0, sl]).then_inc(h_rdy, 1)

                        mult(0)
                        mult(1)
                        h_split(0)
                        mult(2)
                        h_split(1)
                        h_split(2)
                    if isinstance(g, int) and g == 0:
                        v.wait_ge(acc_zero, l + 1)
                    for j in range(2 * NT):
                        a = acc[l][:, j // 2, 512 * (j % 2):512 * (j % 2) + 512]
                        v.wait_ge(down_done, g * 18 + (18 * NG * l + j + 1))
                        v.tensor_tensor(a, a, ps[:, 6 + j % 2, :], ALU.add).then_inc(down_added, 1)

                def run(self):
                    self.body(0, False)
                    with v.Fori(0, NG - 2) as i:
                        chain.enter(i, 5)
                        self.body(i + 1, False)
                    chain.leave(NG - 2)
                    self.body(NG - 1, True)

            f = Ffn(0, U_FFN0, D_DOWN0)
            f.lo_u(0, 0)
            ln_vec("mid0", act_b, from_psum)
            f.run()
            u_lo_at(U_FOUR, None, 0)
            ln_vec("end0", act_b, from_acc(0))

            d_lo_at(D_CHAN, D_CHAN % 2, chan[:, 1, :], chan[:, 0, :], 2 * P)
            u_lo_at(U_FOUR + 1, None, 1)
            for b in range(FB):
                if b:
                    u_lo_at(U_CONV, None, 0)
                for c in range(NCH):
                    v.wait_ge(fi_hi, 3 * b + c + 1)
                    sl = slice(c * CH, (c + 1) * CH)
                    lo(f_in[:, b, 1, sl], ps[:, 3 * b + c, 0:CH], f_in[:, b, 0, sl]).then_inc(bank_free[b], 1)
            cols_of(range(6, 8))
            d_lo_at(D_CTAB, D_CTAB % 2, dw[:, 0, 1, 0:2 * P], dw[:, 0, 0, 0:2 * P], 2 * P)
            for tile in range(NT):
                v.wait_ge(fc_hi, tile + 1)
                lo(f_ch[:, tile, 1, :], ps[:, 6 + tile % 2, :], f_ch[:, tile, 0, :]).then_inc(fc_lo, 1)
            for k in range(16):
                s = (k + 1) % 2
                d_lo_at(D_TAB + k, (D_TAB + k) % 2, dw[:, s, 1, :], dw[:, s, 0, :])
            for b in range(FB):
                for h in range(3):
                    v.wait_ge(pos_hi, 3 * b + h + 1)
                    sl = slice(0, CTX) if h == 0 else slice(CTX + 512 * (h - 1), CTX + 512 * h)
                    i = ps[:, 4 + b, 0:P] if h == 0 else ps[:, 2 * b + h - 1, :]
                    lo(act_a[:, CB + b, 1, sl], i, act_a[:, CB + b, 0, sl]).then_inc(pos_lo, 1)

            v.wait_ge(pads, 2)
            taps6 = par[:, 176:200].rearrange("p (j f) -> p j f", j=4)
            with v.Fori(0, CB // 2) as i:
                chain.enter(i, 7)
                chain(v.tensor_copy(fgrp[:], taps6[:, :, bass.ds(i * 2, 2)]))
                for j in range(2):
                    b = i * 2 + j
                    u_lo_at(*conv_unit(i, 3 * j + 1))
                    u_lo_at(*conv_unit(i, 3 * j + 2))
                    n = conv_unit(i, 3 * j + 1)[0]
                    b0 = 3 * ((3 * j + 1) % 2)
                    for c in range(NCH):
                        v.wait_ge(ch_rdy, b * 3 + (c + 1))
                        v.wait_ge(up_done, n * 3 + (6 + c + 1))
                        for s0, ln, p0 in PIECES[c]:
                            o = v.tensor_tensor(c_p[:, p0:p0 + ln], c_h[:, s0:s0 + ln], ps[:, b0 + c, s0 - c * CH:s0 - c * CH + ln], ALU.mult)
                        o.then_inc(cp_rdy, 1)
                    v.wait_ge(cp_rdy, b * 3 + 6)
                    conv3(c_t, c_p, lambda k: fgrp[:, k, j:j + 1], None)
                    u_lo_at(*conv_unit(i, 3 * j + 3))
                    n = conv_unit(i, 3 * j + 2)[0]
                    b0 = 3 * ((3 * j + 2) % 2)
                    for c in range(NCH):
                        v.wait_ge(up_done, n * 3 + (6 + c + 1))
                        for s0, ln, p0 in PIECES[c]:
                            o = v.tensor_tensor(c_m[:, s0:s0 + ln], c_t[:, p0:p0 + ln], ps[:, b0 + c, s0 - c * CH:s0 - c * CH + ln], ALU.mult)
                        o.then_inc(cm_rdy, 1)
                    for c in range(NCH):
                        v.wait_ge(cm_hi, b * 3 + (c + 1))
                        sl = slice(c * CH, (c + 1) * CH)
                        line = "p a n -> p (a n)"
                        lo(act_a[:, bass.ds(b, 1), 1, sl].rearrange(line), c_m[:, sl], act_a[:, bass.ds(b, 1), 0, sl].rearrange(line)).then_inc(cm_lo, 1)
            chain.leave(CB // 2)
            for k in range(KD):
                wo_lo(1, k, D_OUT1)
            ln_vec("mid1", act_a, from_psum)
            Ffn(1, U_FFN1, D_DOWN1).run()
            ln_vec("end1", None, from_acc(1))

        @block.tensor
        def _(pe):
            PASSES = ((0, 0), (0, 1), (1, 0))

            pe.wait_ge(s_con, 16 * 10)
            for o, rows, i in ((0, 88, 0), (88, 88, 1), (176, 28, 2), (204, 16, 3)):
                pe.transpose(ps[:, 0, o:o + rows], prow[0:rows, i, :], ident[0:rows, 0:rows]).then_inc(setup_t, 1)

            def ada_block(m):
                pe.wait_ge(ada_bank, m + 1)
                for u in range(4):
                    a = 4 * m + u
                    pe.wait_ge(ada_ld[a % ADA_SLOTS], 16 * (a // ADA_SLOTS + 1))
                    for kk in range(2):
                        mm = pe.matmul(ps[0:2, m % 3, :], conds[:, 2 * u + kk, :], ada_w[m >= 16][:, a % ADA_SLOTS, kk, :],
                                       start=(u, kk) == (0, 0), stop=(u, kk) == (3, 1))
                    mm.then_inc(ada_used, 1)

            def cols_mm(ns):
                for n in ns:
                    pe.wait_ge(brow[n % 2], 32 * (n // 2 + 1))
                    if n >= 2:
                        pe.wait_ge(cols_done, n - 1)
                    for k in range(KD):
                        mm = pe.matmul(ps[:, 6 + n % 2, 2 * k:2 * k + 2], bias_row[n % 2][0:3, k * P:(k + 1) * P], con[0:3, C_SELC:C_SELC + 2],
                                       start=True, stop=True)
                    mm.then_inc(brow_mm, 1)

            pe.wait_ge(setup_c, 2)
            for m in range(4):
                ada_block(m)

            def gate(cond, i1):
                for h in range(2):
                    mm = pe.matmul(ps[:, 6 + h, :], con[0:3, C_SELB + P * cond:C_SELB + P * (cond + 1)], ln_u[0:3, 512 * h:512 * (h + 1)],
                                   start=True, stop=True)
                mm.then_inc(gate_mm, 1)

            def ln_turn(tile, i4):
                pe.wait_ge(z_rdy, NT * i4 + tile + 1)
                if tile:
                    pe.wait_ge(mod_done, NT * i4 + tile)
                for k in range(KD):
                    mm = pe.transpose(ps[:, 6 + k // 4, (k % 4) * P:(k % 4 + 1) * P], ln_z[:, k * P:(k + 1) * P], ident)
                mm.then_inc(zt_done, 1)

            def gates(i1):
                pe.wait_ge(gate_ld, 32 * (i1 + 1))
                gate(1, i1)
                pe.wait_ge(gate_rdy, 2 * i1 + 1)
                gate(0, i1)

            def ln_mid(l, kind, src, first_chunk):
                i1, i4 = LN[kind]["i1"], LN[kind]["i4"]

                def project(tile):
                    if tile >= 3:
                        pe.wait_ge(out_evac, NT * i1 + tile - 2)
                    for h in range(2):
                        for k in range(KD):
                            for a, w in PASSES:
                                mm = pe.matmul(ps[:, 2 * (tile % 3) + h, :], src[:, k, a, tile * P:(tile + 1) * P], wo[l][:, k, w, 512 * h:512 * (h + 1)],
                                               start=(k, a, w) == (0, 0, 0), stop=(k, a, w) == (KD - 1, 1, 0))
                    mm.then_inc(out_done, 1)

                project(0)
                gates(i1)
                project(1)
                project(2)
                pe.wait_ge(gate_rdy, 2 * i1 + 2)
                for tile in range(NT):
                    ln_turn(tile, i4)
                    if tile + 3 < NT:
                        project(tile + 3)
                    if tile >= NT - 3:
                        first_chunk(tile - (NT - 3))

            def chunk(out, u_slot, src, c):
                for k in range(KD):
                    for w, a in PASSES:
                        mm = pe.matmul(out, uw[:, u_slot, w, k, :], src[:, k, a, c * CH:(c + 1) * CH],
                                       start=(k, w, a) == (0, 0, 0), stop=(k, w, a) == (KD - 1, 1, 0))
                mm.then_inc(up_done, 1)

            def ln_turns(kind, next_chunk):
                for s in range(NT + 1):
                    for m in ada_steps(kind).get(s, []):
                        ada_block(m)
                    if kind == "in" and s == 1:
                        cols_mm(range(2))
                        pe.wait_ge(cols_done, 2)
                    if s == NT:
                        pe.wait_ge(ada_bank, 3 + 16 if kind == "in" else 3 + 24)
                        next_chunk(0)
                        next_chunk(1)
                    if s:
                        ln_turn(s - 1, LN[kind]["i4"])

            def pool_chunk(n, c):
                if n == 0:
                    pe.wait_ge(act_rdy, 3 * (c + 1))
                if c == 0:
                    pe.wait_ge(u_split, n + 3)
                pe.wait_ge(bank_free[n % 2], 3 * (n // 2) + c + 1)
                chunk(ps[:, 3 * (n % 2) + c, 0:CH], n % 2, act_a, c)

            ln_turns("in", lambda c: pool_chunk(0, c))
            for n in range(U_POOL, U_FFN0):
                for c in range(0 if n else 2, NCH):
                    pool_chunk(n, c)
                if n in (1, 3):
                    cols_mm(range(n + 1, n + 3))

            pe.wait_ge(bank_free[0], 9)
            pe.wait_ge(bank_free[1], 9)
            pe.wait_ge(d_split, D_WPOOL + 2)

            def qkv(tile):
                par2 = tile % 2
                if tile >= 2:
                    pe.wait_ge(qkv_free, tile - 1)
                for k in range(KD):
                    for a, w in PASSES:
                        x = act_a[:, k, a, tile * P:(tile + 1) * P]
                        st, sp_ = (k, a, w) == (0, 0, 0), (k, a, w) == (KD - 1, 1, 0)
                        pe.matmul(ps[:, 2 * par2, :], x, wq[:, k, w, :], start=st, stop=sp_)
                        mm = pe.matmul(ps[:, 2 * par2 + 1, 0:256], x, wkv[:, k, w, :], start=st, stop=sp_)
                mm.then_inc(qkv_done, 1)

            def turn_keys(idx):
                pe.wait_ge(k_lo, idx + 1)
                if idx >= 2:
                    pe.wait_ge(kt_ev, idx - 1)
                for kv in range(NKV):
                    mm = pe.transpose(ps[:, 4 + idx % 2, kv * P:(kv + 1) * P], k4[:, kv, :, :].rearrange("p a d -> p (a d)"), ident)
                mm.then_inc(kt_tr, 1)

            qkv(0)
            qkv(1)
            turn_keys(0)
            turn_keys(1)
            for tile in range(2, NT):
                qkv(tile)
                turn_keys(tile)
            turn_keys(NT)

            def turn_queries(tile, j):
                pe.wait_ge(qs_lo, tile.unit0 + (j + 1))
                for r in range(2):
                    use = ("q", j, r)
                    tile.wait_bank(pe, use)
                    for h in range(2):
                        for a in range(2):
                            mm = pe.transpose(ps[:, 6 + tile.bank(use), (2 * h + a) * P:(2 * h + a + 1) * P],
                                              qs[:, 2 * r + h, a, :, :].rearrange("p b d -> p (b d)"), ident)
                mm.then_inc(qt_tr, 1)

            def first(tile):
                if tile.ctx:
                    pe.wait_ge(qkv_free, NT)
                    pe.wait_ge(kt_ev, NT + 1)
                turn_queries(tile, 0)

            def step(tile, s):
                if has_score(tile, s):
                    h = s + 1
                    j = h // 4
                    if h % 4 == 0:
                        for r in range(2):
                            tile.wait_evac(pe, ("q", j, r))
                    if tile.ctx:
                        if h >= 2:
                            pe.wait_ge(exp_done, h - 1)
                    else:
                        pe.wait_ge(exp_done, tile.head0 + (h - 1))
                    for c in range(3 if tile.nk > 1 else 1):
                        nw = CH if tile.nk > 1 else P
                        k0 = tile.key0 + c * CH
                        for a in range(2):
                            mm = pe.matmul(ps[:, 3 * (h % 2) + c, 0:nw], qt[:, j % 2, h % 4, a, :], kt[:, j % 2, k0:k0 + nw],
                                           start=a == 0, stop=a == 1)
                    mm.then_inc(s_done, 1)
                j = tile.output(s)
                if j is not None:
                    use = ("o", j, 0)
                    tile.wait_bank(pe, use)
                    tile.wait_evac(pe, use, back=1)
                    for a in range(2):
                        for kb in range(tile.nk):
                            mm = pe.matmul(ps[:, 6 + tile.bank(use), :], vhl[:, tile.key0 // P + kb, j % 2, :, :].rearrange("p a d -> p (a d)"),
                                           pt[:, a, kb, :, :].rearrange("p h t -> p (h t)"),
                                           start=(a, kb) == (0, 0), stop=(a, kb) == (1, tile.nk - 1))
                    mm.then_inc(pv_done, 1)
                if has_trans(s):
                    h = s - 2
                    pe.wait_ge(p_rdy, tile.head0 + (h + 1))
                    for r in range(tile.rounds):
                        use = ("t", h, r)
                        tile.wait_bank(pe, use)
                        for b in range(min(3, tile.nk)):
                            mm = pe.transpose(ps[:, 6 + tile.bank(use), b * P:(b + 1) * P], prob[:, h % 4, (3 * r + b) * P:(3 * r + b + 1) * P], ident)
                        mm.then_inc(tr_done, 1)
                if tile.turns(s):
                    turn_queries(tile, (s - 1) // 4 + 1)

            att_steps(pe, step, first)

            pe.wait_ge(d_split, D_WPOOL + 3)
            for g in range(NPG):
                pe.wait_ge(ph_lo, g + 1)
                if g >= 2:
                    pe.wait_ge(mix_ev, g - 1)
                for c in range(NCH):
                    for w, a in PASSES:
                        mm = pe.matmul(ps[:, 3 * (g % 2) + c, 0:CH], wp[:, w, g, :], ph[:, g, a, c * CH:(c + 1) * CH],
                                       start=(w, a) == (0, 0), stop=(w, a) == (1, 0))
                mm.then_inc(mix_done, 1)

            def up_chunk(g, l, u0, b, gate_unit, c):
                if c == 0:
                    pe.wait_ge(u_split, g * 4 + (u0 + 2 * b + gate_unit + 3))
                if gate_unit:
                    pe.wait_ge(h_mul, g * 6 + (66 * l + 3 * b + c + 1))
                else:
                    r = 2 + (NF + 1) * l + b
                    pe.wait_ge(bank_free[0], g * 6 + (3 * r + c + 1))
                chunk(ps[:, 3 * gate_unit + c, 0:CH], gate_unit, act_b if l == 0 else act_a, c)

            def first_up_chunk(l, u0):
                def first(c):
                    pe.wait_ge(act_rdy, NT * (2 * l + 1) + 3 * (c + 1))
                    up_chunk(0, l, u0, 0, 0, c)
                return first

            def ffn_group(g, l, u0, d0, first):
                for b in range(2):
                    for gate_unit in range(2):
                        if first and b == 0 and gate_unit == 0:
                            continue
                        for c in range(NCH):
                            up_chunk(g, l, u0, b, gate_unit, c)
                pe.wait_ge(d_split, g * 2 + (d0 + 4))
                for j in range(2 * NT):
                    tile, h = j // 2, j % 2
                    if h == 0 and tile % 3 == 0:
                        pe.wait_ge(h_rdy, g * 6 + (66 * l + 3 + tile // 3 + 1))
                    pe.wait_ge(down_added, g * 18 + (18 * NG * l + j + 1))
                    for b in range(2):
                        for a, w in PASSES:
                            mm = pe.matmul(ps[:, 6 + h, :], hh[l][:, b, a, tile * P:(tile + 1) * P], dw[:, b, w, 512 * h:512 * (h + 1)],
                                           start=(b, a, w) == (0, 0, 0), stop=(b, a, w) == (1, 1, 0))
                    mm.then_inc(down_done, 1)

            def ffn(l, u0, d0):
                ffn_group(0, l, u0, d0, True)
                with pe.Fori(1, NG) as g:
                    ffn_group(g, l, u0, d0, False)

            def ln_end(kind, next_chunk=None):
                i1, i4 = LN[kind]["i1"], LN[kind]["i4"]
                pe.wait_ge(down_added, 2 + 18 * NG * ((i1 + 1) // 2))
                gates(i1)
                if i4 is not None:
                    pe.wait_ge(gate_rdy, 2 * i1 + 2)
                    ln_turns(kind, next_chunk)

            pe.wait_ge(d_split, D_OUT0 + 4 + 2)
            pe.wait_ge(out_lo, 4)
            pe.wait_ge(mix_lo, NPG)
            pe.wait_ge(m_att, 2 + 2 * NQ)
            ln_mid(0, "mid0", act_b, first_up_chunk(0, U_FFN0))
            ffn(0, U_FFN0, D_DOWN0)

            def four_chunk(b, c):
                if b == 0:
                    pe.wait_ge(act_rdy, 2 * NT + 3 * (c + 1))
                if c == 0:
                    pe.wait_ge(u_split, U_FOUR + b + 3)
                pe.wait_ge(bank_free[b], 3 * (24, 2)[b] + c + 1)
                chunk(ps[:, 3 * b + c, 0:CH], (U_FOUR + b) % 2, act_b, c)

            ln_end("end0", lambda c: four_chunk(0, c))

            for b in range(FB):
                for c in range(0 if b else 2, NCH):
                    four_chunk(b, c)
            pe.wait_ge(d_split, D_CHAN + 3)
            pe.wait_ge(bank_free[0], 78)
            pe.wait_ge(bank_free[1], 12)
            cols_mm(range(6, 8))
            pe.wait_ge(cols_done, 8)
            for tile in range(NT):
                if tile >= 2:
                    pe.wait_ge(fc_lo, tile - 1)
                for b in range(FB):
                    for a, w in PASSES:
                        mm = pe.matmul(ps[:, 6 + tile % 2, 2 * P * b:2 * P * (b + 1)], f_in[:, b, a, tile * P:(tile + 1) * P], chan[:, w, :],
                                       start=(a, w) == (0, 0), stop=(a, w) == (1, 0))
                mm.then_inc(fc_done, 1)

            def f_part(tile, a, b, s):
                return f_ch[:, tile, a, 2 * P * b + P * s:2 * P * b + P * (s + 1)]

            pe.wait_ge(fc_lo, NT)
            pe.wait_ge(d_split, D_CTAB + 3)
            for b in range(FB):
                for s in range(2):
                    for a, w in PASSES:
                        mm = pe.matmul(ps[:, 4 + b, 0:P], f_part(0, a, b, s), dw[:, 0, w, s * P:(s + 1) * P],
                                       start=(s, a, w) == (0, 0, 0), stop=(s, a, w) == (1, 1, 0))
            mm.then_inc(d_used, 1)
            for k in range(16):
                pe.wait_ge(d_split, D_TAB + k + 3)
                for b in range(FB):
                    for h in range(2):
                        for a, w in PASSES:
                            mm = pe.matmul(ps[:, 2 * b + h, :], f_part(1 + k // 2, a, b, k % 2), dw[:, (k + 1) % 2, w, 512 * h:512 * (h + 1)],
                                           start=k == 0 and (a, w) == (0, 0), stop=k == 15 and (a, w) == (1, 0))
                mm.then_inc(d_used, 1)

            pe.wait_ge(pos_lo, 6)
            with pe.Fori(0, CB // 2) as i:
                for e in range(6):
                    j, m = e // 3, e % 3
                    n, _h, slot = conv_unit(i, e)
                    pe.wait_ge(u_split, n + 3)
                    for c in range(NCH):
                        pe.wait_ge((cp_rdy, cm_rdy, ch_rdy)[m], i * 6 + (3 * j + c + 1))
                        chunk(ps[:, 3 * slot + c, 0:CH], slot, act_b, c)

            pe.wait_ge(d_split, D_OUT1 + 4 + 2)
            pe.wait_ge(out_lo, 8)
            pe.wait_ge(cm_lo, 3 * CB)
            ln_mid(1, "mid1", act_a, first_up_chunk(1, U_FFN1))
            ffn(1, U_FFN1, D_DOWN1)
            ln_end("end1")


INS = ["cache_k", "cache_v", "c", "c_ctx", "w_ada", "b_ada", "w_in_even", "q_norm_g", "k_norm_g", "w_pool", "pool_scale",
       "w_in_odd", "conv_w", "conv_b", "w_out", "w_up", "ffn_conv_w", "ffn_conv_b", "w_down", "ln_g", "ln_b"]


def kernel(**inputs):
    import concourse.bacc as _bacc
    from concourse.bass_utils import run_bass_kernel_spmd as _run

    nc = _bacc.Bacc("TRN2", target_bir_lowering=False, num_devices=1, dynamic_dma_scratch_size=1024)
    host = {name: np.ascontiguousarray(inputs[name]) for name in INS}
    host["x_all"] = np.concatenate([np.asarray(inputs["x_prompt"])[0], np.asarray(inputs["x_sample"])[0]], 0)
    host.update(constants())
    t = {name: nc.dram_tensor(f"in_{name}", a.shape, F32, kind="ExternalInput").ap() for name, a in host.items()}
    outs = {"y_all": (TOK, D), "new_k": (1, 1, CTX, NKV, HD), "new_v": (1, 1, CTX, NKV, HD)}
    for name, shape in outs.items():
        t[name] = nc.dram_tensor(f"out_{name}", shape, F32, kind="ExternalOutput").ap()
    t["xs"] = nc.dram_tensor("xs", (3, TOK, D), F32, kind="Internal").ap()
    t["ada"] = nc.dram_tensor("ada", (2, 2, 6 * D), F32, kind="Internal").ap()
    build(nc, t)
    r = _run(nc, [{f"in_{name}": a for name, a in host.items()}], core_ids=[0]).results[0]
    y = r["out_y_all"]
    return (y[:CTX].reshape(1, CTX, D), y[CTX:].reshape(1, LAT, D), r["out_new_k"], r["out_new_v"])
```
